# Optimizing a Trainium2 kernel written in Bass

```python
import math
import jax, jax.numpy as jnp
from jax import lax
import numpy as np

D_MODEL = 1024
BATCH = 1
SEQ = 512
DEPTH = 1
DEC_BATCH = 1
DEC_SEQ = 64
PAST_LEN = 512

CHUNK = 64
EPS = 1e-6
MIX_W = D_MODEL
SSD_W = MIX_W // 2
S5_W = MIX_W - SSD_W
SSD_HEAD_DIM = 64
SSD_HEADS = SSD_W // SSD_HEAD_DIM
SSD_GROUPS = 2
SSD_STATE = 128
CONV_K = 4
CONV_CH = SSD_W + 2 * SSD_GROUPS * SSD_STATE
S5_GROUP_CH = 16
S5_GROUPS = S5_W // S5_GROUP_CH
S5_STATE = 64
N_PROJ = SSD_W + CONV_CH + SSD_HEADS + S5_W
MEM_LEN = 256
X_HEADS = 4
X_HEAD_DIM = D_MODEL // X_HEADS
N_EXPERT_GROUPS = 4
EXPERTS_PER_GROUP = 8
N_EXPERTS = N_EXPERT_GROUPS * EXPERTS_PER_GROUP
TOP_K_INNER = 2
EXPERT_FF = 256

kernel_name = "hymba_ssd_s5_memxattn_hmoe_stream_step"

def rmsnorm(x, g):
    xf = x.astype(jnp.float32)
    y = xf * lax.rsqrt(jnp.mean(xf * xf, axis=-1, keepdims=True) + EPS)
    return (y * g.astype(jnp.float32)).astype(x.dtype)

def segsum(a):
    t = a.shape[-1]
    cs = jnp.cumsum(a, axis=-1)
    diff = cs[..., :, None] - cs[..., None, :]
    mask = jnp.tril(jnp.ones((t, t), dtype=bool))
    return jnp.where(mask, diff, -jnp.inf)

def ssd_scan(xdt, a, bm, cm, h0, q):
    bsz, L, H, P = xdt.shape
    nc = L // q
    xc = xdt.reshape(bsz, nc, q, H, P)
    bc = bm.reshape(bsz, nc, q, H, -1)
    cc = cm.reshape(bsz, nc, q, H, -1)
    ac = a.reshape(bsz, nc, q, H).transpose(0, 3, 1, 2)
    a_cs = jnp.cumsum(ac, axis=-1)
    scores = jnp.einsum("bclhn,bcshn->bhcls", cc, bc) * jnp.exp(segsum(ac))
    y_diag = jnp.einsum("bhcls,bcshp->bclhp", scores, xc)
    decay_to_end = jnp.exp(a_cs[..., -1:] - a_cs)
    chunk_states = jnp.einsum("bclhn,bhcl,bclhp->bchpn", bc, decay_to_end, xc)
    chunk_states = jnp.concatenate([h0[:, None], chunk_states], axis=1)
    chunk_decay = jnp.exp(segsum(jnp.pad(a_cs[..., -1], ((0, 0), (0, 0), (1, 0)))))
    states = jnp.einsum("bhzc,bchpn->bzhpn", chunk_decay, chunk_states)
    y_off = jnp.einsum("bclhn,bchpn,bhcl->bclhp", cc, states[:, :-1], jnp.exp(a_cs))
    return (y_diag + y_off).reshape(bsz, L, H, P), states[:, -1]

def causal_conv(xbc, conv_st, w, b):
    L = xbc.shape[1]
    xpad = jnp.concatenate([conv_st.astype(xbc.dtype), xbc], axis=1)
    out = b + w[0] * xpad[:, 0:L]
    for k in range(1, CONV_K):
        out = out + w[k] * xpad[:, k:k + L]
    return jax.nn.silu(out), xpad[:, L:]

def ssd_mixer(z, xbc, dt_raw, conv_st, ssd_st, p):
    bsz, L, _ = z.shape
    f32 = jnp.float32
    xbc, new_conv = causal_conv(xbc, conv_st, p["conv_w"], p["conv_b"])
    xbc = xbc.astype(f32)
    xs, bm, cm = jnp.split(xbc, [SSD_W, SSD_W + SSD_GROUPS * SSD_STATE], axis=-1)
    xs = xs.reshape(bsz, L, SSD_HEADS, SSD_HEAD_DIM)
    rep = SSD_HEADS // SSD_GROUPS
    bm = jnp.repeat(bm.reshape(bsz, L, SSD_GROUPS, SSD_STATE), rep, axis=2)
    cm = jnp.repeat(cm.reshape(bsz, L, SSD_GROUPS, SSD_STATE), rep, axis=2)
    dt = jax.nn.softplus(dt_raw.astype(f32) + p["dt_bias"].astype(f32))
    a = -jnp.exp(p["a_log"].astype(f32))
    q = math.gcd(min(CHUNK, L), L)
    y, new_ssd = ssd_scan(xs * dt[..., None], dt * a, bm, cm, ssd_st.astype(f32), q)
    y = y + p["d_skip"].astype(f32)[:, None] * xs
    y = y.reshape(bsz, L, SSD_W) * jax.nn.silu(z.astype(f32))
    y = rmsnorm(y, p["ssd_norm"])
    return y, new_conv, new_ssd

def _complex_affine_combine(e1, e2):
    a1r, a1i, b1r, b1i = e1
    a2r, a2i, b2r, b2i = e2
    return (a1r * a2r - a1i * a2i, a1r * a2i + a1i * a2r,
            a2r * b1r - a2i * b1i + b2r, a2r * b1i + a2i * b1r + b2i)

def s5_mixer(u, h_re, h_im, p):
    bsz, L, _ = u.shape
    f32 = jnp.float32
    uf = u.astype(f32).reshape(bsz, L, S5_GROUPS, S5_GROUP_CH)
    a_re, a_im = p["s5_a_re"].astype(f32), p["s5_a_im"].astype(f32)
    dt = jnp.exp(p["s5_log_dt"].astype(f32))[:, None]
    mag = jnp.exp(a_re * dt)
    lam_re, lam_im = mag * jnp.cos(a_im * dt), mag * jnp.sin(a_im * dt)
    den = a_re * a_re + a_im * a_im
    f_re = ((lam_re - 1.0) * a_re + lam_im * a_im) / den
    f_im = (lam_im * a_re - (lam_re - 1.0) * a_im) / den
    b_re, b_im = p["s5_b_re"].astype(f32), p["s5_b_im"].astype(f32)
    bb_re = f_re[..., None] * b_re - f_im[..., None] * b_im
    bb_im = f_re[..., None] * b_im + f_im[..., None] * b_re
    bu_re = jnp.einsum("blgc,gnc->blgn", uf, bb_re)
    bu_im = jnp.einsum("blgc,gnc->blgn", uf, bb_im)
    h_re, h_im = h_re.astype(f32), h_im.astype(f32)
    bu_re = bu_re.at[:, 0].add(lam_re * h_re - lam_im * h_im)
    bu_im = bu_im.at[:, 0].add(lam_re * h_im + lam_im * h_re)
    lam_re_t = jnp.broadcast_to(lam_re, bu_re.shape)
    lam_im_t = jnp.broadcast_to(lam_im, bu_im.shape)
    _, _, s_re, s_im = lax.associative_scan(
        _complex_affine_combine, (lam_re_t, lam_im_t, bu_re, bu_im), axis=1)
    y = (jnp.einsum("blgn,gcn->blgc", s_re, p["s5_c_re"].astype(f32))
         - jnp.einsum("blgn,gcn->blgc", s_im, p["s5_c_im"].astype(f32))
         + p["s5_d"].astype(f32) * uf).reshape(bsz, L, S5_W)
    y = jax.nn.gelu(y)
    y = y * jax.nn.sigmoid(y @ p["s5_w_glu"].astype(f32))
    return y, s_re[:, -1], s_im[:, -1]

def memory_kv(mem, g, w_k, w_v):
    bsz, m, _ = mem.shape
    mn = rmsnorm(mem, g)
    k = (mn @ w_k).reshape(bsz, m, X_HEADS, X_HEAD_DIM)
    v = (mn @ w_v).reshape(bsz, m, X_HEADS, X_HEAD_DIM)
    return k, v

def cross_attn(x, mem_k, mem_v, w_q, w_o):
    bsz, L, _ = x.shape
    f32 = jnp.float32
    q = (x @ w_q).reshape(bsz, L, X_HEADS, X_HEAD_DIM)
    s = jnp.einsum("blhd,bmhd->bhlm", q.astype(f32), mem_k.astype(f32)) * (X_HEAD_DIM ** -0.5)
    pr = jax.nn.softmax(s, axis=-1)
    o = jnp.einsum("bhlm,bmhd->blhd", pr, mem_v.astype(f32)).reshape(bsz, L, D_MODEL)
    return o.astype(x.dtype) @ w_o

def hmoe(x, p):
    bsz, L, _ = x.shape
    f32 = jnp.float32
    t = x.reshape(bsz * L, D_MODEL)
    g_logits = (t @ p["w_router_group"]).astype(f32) + p["b_router_group"].astype(f32)
    g_idx = jnp.argmax(g_logits, axis=-1)
    g_onehot = jax.nn.one_hot(g_idx, N_EXPERT_GROUPS, dtype=f32)
    g_prob = jnp.sum(jax.nn.softmax(g_logits, axis=-1) * g_onehot, axis=-1)
    e_logits = (jnp.einsum("td,dge->tge", t, p["w_router_expert"]).astype(f32)
                + p["b_router_expert"].astype(f32))
    e_logits = jnp.einsum("tge,tg->te", e_logits, g_onehot)
    top_v, top_i = lax.top_k(e_logits, TOP_K_INNER)
    gates = jax.nn.softmax(top_v, axis=-1) * g_prob[:, None]
    expert_id = g_idx[:, None] * EXPERTS_PER_GROUP + top_i
    combine = jnp.einsum("tk,tke->te", gates,
                         jax.nn.one_hot(expert_id, N_EXPERTS, dtype=f32)).astype(x.dtype)
    out = jnp.zeros_like(t)
    for e in range(N_EXPERTS):
        hid = jax.nn.silu(t @ p["w_gate"][e]) * (t @ p["w_up"][e])
        out = out + (hid @ p["w_down"][e]) * combine[:, e:e + 1]
    return out.reshape(bsz, L, D_MODEL)

def block(h, conv_st, ssd_st, s5r_st, s5i_st, mem_k, mem_v, p):
    proj = rmsnorm(h, p["norm_mix"]) @ p["w_in"]
    z, xbc, dt_raw, u = jnp.split(proj, [SSD_W, SSD_W + CONV_CH, SSD_W + CONV_CH + SSD_HEADS], axis=-1)
    y_ssd, new_conv, new_ssd = ssd_mixer(z, xbc, dt_raw, conv_st, ssd_st, p)
    y_s5, new_re, new_im = s5_mixer(u, s5r_st, s5i_st, p)
    mix = jnp.concatenate([y_ssd.astype(h.dtype), y_s5.astype(h.dtype)], axis=-1)
    h = h + mix @ p["w_out"]
    h = h + cross_attn(rmsnorm(h, p["norm_x"]), mem_k, mem_v, p["w_q"], p["w_o"])
    h = h + hmoe(rmsnorm(h, p["norm_ffn"]), p)
    return h, (new_conv, new_ssd.astype(h.dtype), new_re.astype(h.dtype), new_im.astype(h.dtype))

def setup_inputs(seed: int = 0) -> dict:
    key = jax.random.key(seed)
    ks = iter(jax.random.split(key, 64))
    f32 = jnp.float32

    def nrm(shape, scale):
        return scale * jax.random.normal(next(ks), shape, f32)

    def gain(shape):
        return 1.0 + 0.02 * jax.random.normal(next(ks), shape, f32)

    def unif(shape, lo, hi):
        return jax.random.uniform(next(ks), shape, f32, lo, hi)

    dt0 = jnp.exp(unif((DEPTH, SSD_HEADS), math.log(1e-3), math.log(1e-1)))
    return {
        "x_prompt": nrm((BATCH, SEQ, D_MODEL), 1.0),
        "x_sample": nrm((DEC_BATCH, DEC_SEQ, D_MODEL), 1.0),
        "cache_conv": nrm((DEPTH, DEC_BATCH, CONV_K - 1, CONV_CH), 1.0),
        "state_ssd": nrm((DEPTH, DEC_BATCH, SSD_HEADS, SSD_HEAD_DIM, SSD_STATE), 0.1),
        "state_s5_re": nrm((DEPTH, DEC_BATCH, S5_GROUPS, S5_STATE), 0.1),
        "state_s5_im": nrm((DEPTH, DEC_BATCH, S5_GROUPS, S5_STATE), 0.1),
        "cache_mem_k": nrm((DEPTH, DEC_BATCH, MEM_LEN, X_HEADS, X_HEAD_DIM), 1.0),
        "cache_mem_v": nrm((DEPTH, DEC_BATCH, MEM_LEN, X_HEADS, X_HEAD_DIM), 1.0),
        "mem_prompt": nrm((BATCH, MEM_LEN, D_MODEL), 1.0),
        "norm_mix": gain((DEPTH, D_MODEL)),
        "w_in": nrm((DEPTH, D_MODEL, N_PROJ), D_MODEL ** -0.5),
        "conv_w": nrm((DEPTH, CONV_K, CONV_CH), CONV_K ** -0.5),
        "conv_b": nrm((DEPTH, CONV_CH), 0.02),
        "dt_bias": dt0 + jnp.log(-jnp.expm1(-dt0)),
        "a_log": jnp.log(unif((DEPTH, SSD_HEADS), 1.0, 16.0)),
        "d_skip": gain((DEPTH, SSD_HEADS)),
        "ssd_norm": gain((DEPTH, SSD_W)),
        "s5_a_re": -0.5 + nrm((DEPTH, S5_GROUPS, S5_STATE), 0.01),
        "s5_a_im": math.pi * jnp.arange(S5_STATE, dtype=f32) + nrm((DEPTH, S5_GROUPS, S5_STATE), 0.01),
        "s5_log_dt": unif((DEPTH, S5_GROUPS), math.log(1e-3), math.log(1e-1)),
        "s5_b_re": nrm((DEPTH, S5_GROUPS, S5_STATE, S5_GROUP_CH), (2 * S5_GROUP_CH) ** -0.5),
        "s5_b_im": nrm((DEPTH, S5_GROUPS, S5_STATE, S5_GROUP_CH), (2 * S5_GROUP_CH) ** -0.5),
        "s5_c_re": nrm((DEPTH, S5_GROUPS, S5_GROUP_CH, S5_STATE), S5_STATE ** -0.5),
        "s5_c_im": nrm((DEPTH, S5_GROUPS, S5_GROUP_CH, S5_STATE), S5_STATE ** -0.5),
        "s5_d": gain((DEPTH, S5_GROUPS, S5_GROUP_CH)),
        "s5_w_glu": nrm((DEPTH, S5_W, S5_W), S5_W ** -0.5),
        "w_out": nrm((DEPTH, MIX_W, D_MODEL), MIX_W ** -0.5),
        "norm_x": gain((DEPTH, D_MODEL)),
        "norm_mem": gain((DEPTH, D_MODEL)),
        "w_q": nrm((DEPTH, D_MODEL, D_MODEL), D_MODEL ** -0.5),
        "w_k": nrm((DEPTH, D_MODEL, D_MODEL), D_MODEL ** -0.5),
        "w_v": nrm((DEPTH, D_MODEL, D_MODEL), D_MODEL ** -0.5),
        "w_o": nrm((DEPTH, D_MODEL, D_MODEL), D_MODEL ** -0.5),
        "norm_ffn": gain((DEPTH, D_MODEL)),
        "w_router_group": nrm((DEPTH, D_MODEL, N_EXPERT_GROUPS), D_MODEL ** -0.5),
        "b_router_group": nrm((DEPTH, N_EXPERT_GROUPS), 0.01),
        "w_router_expert": nrm((DEPTH, D_MODEL, N_EXPERT_GROUPS, EXPERTS_PER_GROUP), D_MODEL ** -0.5),
        "b_router_expert": nrm((DEPTH, N_EXPERT_GROUPS, EXPERTS_PER_GROUP), 0.01),
        "w_gate": nrm((DEPTH, N_EXPERTS, D_MODEL, EXPERT_FF), D_MODEL ** -0.5),
        "w_up": nrm((DEPTH, N_EXPERTS, D_MODEL, EXPERT_FF), D_MODEL ** -0.5),
        "w_down": nrm((DEPTH, N_EXPERTS, EXPERT_FF, D_MODEL), EXPERT_FF ** -0.5),
        "norm_final": gain((D_MODEL,)),
    }

def reference(x_prompt, x_sample, cache_conv, state_ssd, state_s5_re, state_s5_im,
              cache_mem_k, cache_mem_v, mem_prompt,
              norm_mix, w_in, conv_w, conv_b, dt_bias, a_log, d_skip, ssd_norm,
              s5_a_re, s5_a_im, s5_log_dt, s5_b_re, s5_b_im, s5_c_re, s5_c_im, s5_d, s5_w_glu,
              w_out, norm_x, norm_mem, w_q, w_k, w_v, w_o, norm_ffn,
              w_router_group, b_router_group, w_router_expert, b_router_expert,
              w_gate, w_up, w_down, norm_final):
    bp = x_prompt.shape[0]
    hp, hs = x_prompt, x_sample
    new_p, new_s = [], []
    for l in range(DEPTH):
        p = {
            "norm_mix": norm_mix[l], "w_in": w_in[l], "conv_w": conv_w[l], "conv_b": conv_b[l],
            "dt_bias": dt_bias[l], "a_log": a_log[l], "d_skip": d_skip[l], "ssd_norm": ssd_norm[l],
            "s5_a_re": s5_a_re[l], "s5_a_im": s5_a_im[l], "s5_log_dt": s5_log_dt[l],
            "s5_b_re": s5_b_re[l], "s5_b_im": s5_b_im[l], "s5_c_re": s5_c_re[l], "s5_c_im": s5_c_im[l],
            "s5_d": s5_d[l], "s5_w_glu": s5_w_glu[l], "w_out": w_out[l],
            "norm_x": norm_x[l], "w_q": w_q[l], "w_o": w_o[l], "norm_ffn": norm_ffn[l],
            "w_router_group": w_router_group[l], "b_router_group": b_router_group[l],
            "w_router_expert": w_router_expert[l], "b_router_expert": b_router_expert[l],
            "w_gate": w_gate[l], "w_up": w_up[l], "w_down": w_down[l],
        }
        mk_p, mv_p = memory_kv(mem_prompt, norm_mem[l], w_k[l], w_v[l])
        zero_conv = jnp.zeros((bp, CONV_K - 1, CONV_CH), hp.dtype)
        zero_ssd = jnp.zeros((bp, SSD_HEADS, SSD_HEAD_DIM, SSD_STATE), jnp.float32)
        zero_s5 = jnp.zeros((bp, S5_GROUPS, S5_STATE), jnp.float32)
        hp, st_p = block(hp, zero_conv, zero_ssd, zero_s5, zero_s5, mk_p, mv_p, p)
        hs, st_s = block(hs, cache_conv[l], state_ssd[l], state_s5_re[l], state_s5_im[l],
                         cache_mem_k[l], cache_mem_v[l], p)
        new_p.append(st_p + (mk_p, mv_p))
        new_s.append(st_s)
    y_prompt = rmsnorm(hp, norm_final)
    y_sample = rmsnorm(hs, norm_final)
    conv_p, ssd_p, s5_re_p, s5_im_p, mem_k_p, mem_v_p = [jnp.stack(a) for a in zip(*new_p)]
    conv_s, ssd_s, s5_re_s, s5_im_s = [jnp.stack(a) for a in zip(*new_s)]
    return (y_prompt, y_sample, conv_p, ssd_p, s5_re_p, s5_im_p, mem_k_p, mem_v_p,
            conv_s, ssd_s, s5_re_s, s5_im_s)


_drawn_inputs = setup_inputs


def setup_inputs(seed=0):
    import zlib

    import numpy as np

    out = dict(_drawn_inputs(seed))
    spreads = {}
    factors = {'d_skip': 81.697,
     's5_a_re': 58.032,
     's5_d': 4.021,
     'norm_x': 8.0,
     'norm_mem': 2.729,
     'b_router_group': 16.965,
     'b_router_expert': 11.374,
     'norm_final': 24.222,
     's5_c_re': 3.119,
     's5_c_im': 3.01,
     'norm_ffn': 3.338}
    for name, (base, spread) in spreads.items():
        noise = np.random.default_rng([zlib.crc32(name.encode()), seed]).standard_normal(out[name].shape)
        drawn = base * np.exp(spread * noise) if base else spread * noise
        out[name] = __import__('jax').numpy.asarray(drawn.astype(out[name].dtype))
    for name, factor in factors.items():
        out[name] = (out[name] * factor).astype(out[name].dtype)
    return out
```

```python
from contextlib import ExitStack

import concourse.bass as bass
from concourse import mybir

ALU = mybir.AluOpType
ACT = mybir.ActivationFunctionType
AX = mybir.AxisListType
F32 = mybir.dt.float32
I32 = mybir.dt.int32
U32 = mybir.dt.uint32

P = 128
D = 1024
KD = D // P
NP, NS = 512, 64
T = NP + NS
TOK = [(0, 128), (128, 128), (256, 128), (384, 128), (512, 64)]
NT = len(TOK)
HALF = T // 2
EPS = 1e-6
SSD_W, S5_W = 512, 512
HEADS, HD, NST = 8, 64, 128
CONV_K, CONV_CH = 4, 1024
N_PROJ = 2056
COL_Z, COL_XBC, COL_DT, COL_U = 0, 512, 1536, 1544
GRP, GC, SN = 32, 16, 64
Q8 = 8
NJ = T // Q8
PAIRS = GRP // 2
SUP = NJ // 8
MEM, XH, XD = 256, 4, 256
NG, EG, NE, FF = 4, 8, 32, 256
CW = 256
SLOTS = 6
CONV_COLS = 3 + NP + 3 + NS
CONV_OUT = CONV_COLS - 3
SAMPLE_COL = NP + 3
XC = [0, 128, 256, 384, SAMPLE_COL]
CAP = 80
PASSES = -(-T // CAP)
SKIP = float(1 << 20)
O_STEP = NT + 2
Q_FILL = {0: [(4, 0), (5, 0)], 1: [(6, 0)], 2: [(7, 0)], 3: [(4, 1)], 4: [(5, 1)], 5: [(6, 1)], 6: [(7, 1)]}
Y_POOL = 3
ROUTE_PARTS = ((0, T // 2), (T // 2, 4 * P), (4 * P, T))
Q_FIRST = [(m, h) for m in range(4) for h in range(2)][1:]
TWO_PI = 6.283185307179586
PI_A, PI_B, PI_C = 6.28125, 0.0019350051879882812, 3.0199159819e-07
MAGIC = 12582912.0

IN = ["x_prompt", "x_sample", "cache_conv", "state_ssd", "state_s5_re", "state_s5_im",
      "cache_mem_k", "cache_mem_v", "mem_prompt", "norm_mix", "w_in", "conv_w", "conv_b", "dt_bias",
      "a_log", "d_skip", "ssd_norm", "s5_a_re", "s5_a_im", "s5_log_dt", "s5_b_re", "s5_b_im",
      "s5_c_re", "s5_c_im", "s5_d", "s5_w_glu", "w_out", "norm_x", "norm_mem", "w_q", "w_k", "w_v",
      "w_o", "norm_ffn", "w_router_group", "b_router_group", "w_router_expert", "b_router_expert",
      "w_gate", "w_up", "w_down", "norm_final"]
OUT = [("y_prompt", (1, NP, D)), ("y_sample", (1, NS, D)), ("conv_p", (1, 1, 3, CONV_CH)),
       ("ssd_p", (1, 1, HEADS, HD, NST)), ("s5_re_p", (1, 1, GRP, SN)), ("s5_im_p", (1, 1, GRP, SN)),
       ("mem_k_p", (1, 1, MEM, XH, XD)), ("mem_v_p", (1, 1, MEM, XH, XD)),
       ("conv_s", (1, 1, 3, CONV_CH)), ("ssd_s", (1, 1, HEADS, HD, NST)),
       ("s5_re_s", (1, 1, GRP, SN)), ("s5_im_s", (1, 1, GRP, SN))]


def plan_psum():
    plan = []

    def add(stage, who, *index):
        plan.append((stage, index, who))

    for t in range(2):
        for h in range(2):
            add("xT", "act", t, h)
    add("vec", "dve")
    add("s5par", "dve")
    for h in range(2):
        add("xT", "act", 2, h)
    add("u", "act", 0, 0)
    for ri in range(2):
        add("cT", "act", ri)
    add("u", "act", 1, 0)
    for t in (3, 4):
        for h in range(2):
            add("xT", "act", t, h)
    for m in range(2, 4):
        add("u", "act", m, 0)
    for m in range(4):
        add("u", "act", m, 1)
    for b in range(8):
        add("wT", "dve" if b % 2 else "act", b)
    for i in range(4):
        for h in range(2):
            add("uj", "act", i, h)
        add("z", "act", i // 2, i % 2)
        for h in range(2):
            add("ug", "dve", i, h)
    for b in range(8):
        add("v", "dve", b)
    for b in range(4):
        add("tap", "act", b)
    add("dtf", "act", 0)
    add("dtf", "act", 1)
    add("dt", "dve")
    for m in range(8):
        for h in range(2):
            add("xbc", "act", m, h)
    for m in range(2, 4):
        for h in range(2):
            add("z", "act", m, h)
    for i in range(4):
        for g2 in range(2):
            add("y", "act", i, g2)
        for h in range(2):
            add("yT", "dve", i, h)
    for m in range(4):
        for h in range(2):
            add("glu", "act", m, h)

    add("s5fin", "act")
    for b in range(2):
        for h in range(2):
            add("convT", "act", b, h)

    def prep(c):
        add("tot", "act", c)
        add("cs", "act", c)
        for hg in range(2):
            add("seg", "act", c, hg)
        add("cb", "dve", c)
        add("xs", "dve", c)
        add("bt", "act", c)

    add("stin", "dve")
    prep(0)
    for t in range(2):
        for h in range(2):
            add("memT", "act", t, h)
    for c in range(NT):
        if c + 1 < NT:
            prep(c + 1)
        add("yoff", "dve", c)
        add("ydiag", "dve", c)
        add("state", "dve", c)
        if c < 4:
            add("v_mem", "act", c, 0)
            add("v_mem", "act", c, 1)
    for s in range(2):
        add("stout", "act", s)
    for c in range(2):
        add("k_mem", "act", c, 0)
        add("k_mem", "act", c, 1)
    add("ssq", "dve")
    add("k_mem", "act", 2, 0)
    add("k_mem", "act", 2, 1)
    add("rbc", "dve", 0)
    add("rbc", "dve", 1)
    add("k_mem", "act", 3, 0)
    add("k_mem", "act", 3, 1)
    for b in range(4):
        add("kT", "act", b)
    for t in range(NT):
        for h in range(2):
            add("out", "dve", t, h)
        if t >= 1:
            for h in range(2):
                add("hT", "act", t - 1, h)
    for b in range(4):
        add("ksT", "act", b)
    add("q", "act", 0, 0)
    for h in range(2):
        add("hT", "act", NT - 1, h)
    for m, h in Q_FIRST:
        add("q", "act", m, h)

    def o_tile(t):
        for h in range(2):
            add("o", "dve", t, h)
        if t >= 1:
            for h in range(2):
                add("fT", "act", t - 1, h)

    for n in range(2 * NT + 1):
        if n >= 1:
            add("pT", "act", n - 1)
        if n < 2 * NT:
            add("score", "act", n)
        if n >= 1:
            add("pv", "dve", n - 1)
        for m, h in Q_FILL.get(n, ()):
            add("q", "act", m, h)
        if n >= O_STEP:
            o_tile(n - O_STEP)
    o_tile(NT - 1)
    add("routef", "act", 0)
    for h in range(2):
        add("fT", "act", NT - 1, h)
    add("routef", "act", 1)
    add("routef", "act", 2)
    add("route", "dve")
    add("rank", "dve")
    return plan


def build(nc, a, o):
    plan = plan_psum()
    job, rank, count = {}, {}, {"act": 0, "dve": 0}
    for j, (stage, index, who) in enumerate(plan):
        count[who] += 1
        job[(stage,) + index] = j
        rank[j] = (who, count[who])

    def dram(name, pattern, **k):
        return a[name].rearrange(pattern, **k)

    xf_dram = nc.dram_tensor("ffn_rows", (T, D), F32).ap()
    y2_dram = nc.dram_tensor("expert_rows", (2 * T, D), F32).ap()

    with ExitStack() as ctx:
        def sb(name, shape, dt=F32):
            return ctx.enter_context(nc.sbuf_tensor(name, shape, dt))

        def sem(name):
            return ctx.enter_context(nc.semaphore(name))

        ring = sb("weight_ring", [P, SLOTS, 8, CW])
        act_a = sb("act_a", [P, KD * T])
        act_b = sb("act_b", [P, KD * T])
        gain = sb("gain_rows", [P, 2, D])
        conv = sb("conv_io", [P, 8 * CONV_COLS])
        reg_r = sb("region_r", [P, 4096])
        reg_t = sb("region_t", [P, 4096])
        reg_g = sb("region_g", [P, 4608])
        reg_u = sb("region_u", [P, 5120])
        rows = sb("row_stage", [P, 3, D])
        ident = sb("ident", [P, P])
        tri_le = sb("tri_le", [P, P])
        tri_gt = sb("tri_gt", [P, P])
        tri_lt = sb("tri_lt", [P, P])
        ones = sb("ones", [P, P])
        vecT = sb("vec_t", [P, 8, 9])
        w_dt = sb("w_dt", [P, KD, HEADS])
        w_rt = sb("w_router", [P, KD, NG + NE])
        b_rt = sb("b_router", [P, NG + NE])
        dt_b = sb("dt_bias_rows", [P, HEADS])
        a_lg = sb("a_log_rows", [P, HEADS])
        dsk_rows = sb("d_skip_rows", [P, HEADS])
        dsk = sb("d_skip_cols", [P, 4])
        s5d = sb("s5_d_cols", [32, PAIRS])
        i16 = sb("ident16", [32, GC])
        dti = sb("s5_d_ident", [32, PAIRS * GC])
        dtt = sb("dt_tmp", [P, 7, NT * HEADS])
        dt_v = sb("dt_values", [P, NT, HEADS])
        da_v = sb("da_values", [P, NT, HEADS])
        expo = sb("chunk_decay", [P, 2, 16])
        powr = sb("lam_pow_re", [P, 9, PAIRS])
        powi = sb("lam_pow_im", [P, 9, PAIRS])
        supr = sb("lam8_pow_re", [P, 8, PAIRS])
        supi = sb("lam8_pow_im", [P, 8, PAIRS])
        l8a = sb("lam8_same", [P, 2 * PAIRS])
        l8b = sb("lam8_cross", [P, 2 * PAIRS])
        s5p = sb("s5_params", [P, 5, PAIRS])
        s5s = sb("s5_scratch", [P, 20, PAIRS])
        s5f = sb("s5_final", [P, 4, PAIRS])
        stat = sb("norm_stats", [P, 22, 18])
        sstat = sb("ssd_norm_stats", [P, 4, NT])
        amax = sb("score_max", [P, 2 * NT, 2])
        asum = sb("prob_sum", [P, 2 * NT, 2])
        arec = sb("prob_rec", [P, 2 * NT, 2])

        xT = act_a[:, :].rearrange("p (k t) -> p k t", k=KD)
        mix = act_b[:, :].rearrange("p (k t) -> p k t", k=KD)
        uT = mix[:, 4:8, :]
        xbc = conv[:, :].rearrange("p (k t) -> p k t", k=8)

        def view(reg, off, *shape):
            n = 1
            for s in shape:
                n *= s
            v = reg[:, off:off + n]
            if len(shape) == 2:
                return v.rearrange("p (a b) -> p a b", a=shape[0])
            if len(shape) == 3:
                return v.rearrange("p (a b c) -> p a b c", a=shape[0], b=shape[1])
            if len(shape) == 4:
                return v.rearrange("p (a b c d) -> p a b c d", a=shape[0], b=shape[1], c=shape[2])
            return v

        c_rows = view(reg_t, 0, 2, 4, 2, SN)
        b_raw = view(reg_t, 1024, 2, PAIRS, GC)
        p_rows = view(reg_t, 1536, 5, 128)
        ld_rows = view(reg_t, 1536 + 640, 2)
        s5d_rows = view(reg_t, 1536 + 642, 2 * GC)
        vec_rows = view(reg_u, 0, D)
        prod_a = act_b[:, 0:2304]
        prod_b = conv[:, 0:2304]
        bd = view(conv, 2304, 2, PAIRS, 32)
        c_t = view(conv, 3328, 3, PAIRS, GC)
        bb = view(conv, 4096, 2, PAIRS, GC)
        R = view(reg_r, 0, 2, PAIRS, 8, GC)
        G = view(reg_g, 0, 2, PAIRS, 9 * GC)
        WT = view(reg_t, 0, PAIRS, 2, P)
        Tm = view(reg_t, 0, GRP, P)
        Uj = view(reg_u, 0, 2, 8, P)
        U = view(reg_u, 2048, GRP, NJ)
        tap = view(reg_u, 0, PAIRS, P)
        Yj = view(reg_u, 0, 2, 8, P)
        sig = view(reg_u, 2048, 4, T)
        SS = view(reg_r, 0, 2 * PAIRS, NJ + 1)
        SSc = SS[:, :, 1:NJ + 1].rearrange("p a (s i) -> p a s i", i=8)
        h1 = view(reg_r, 2336, 2 * PAIRS, SUP)
        h2 = view(reg_r, 2624, 2 * PAIRS, SUP)
        h3 = view(reg_r, 2912, 2 * PAIRS, SUP)
        dtT = rows[0:HEADS, 0, 0:T]
        cv = [reg_u[:, 4352:4352 + CONV_OUT], rows[:, 2, 0:CONV_OUT]]
        s5row = view(reg_u, 4352, 4, P)
        conv_rows = view(reg_g, 0, 2, CONV_CH)
        ssd_buf = [reg_r, act_a]
        XDT = [view(r, 0, HEADS, HD) for r in ssd_buf]
        XDE = [view(r, 512, HEADS, HD) for r in ssd_buf]
        DU = [view(r, 1024, HEADS, P) for r in ssd_buf]
        MM = [view(r, 2048, HEADS, P) for r in ssd_buf]
        CB = [view(r, 3072, 2, P) for r in ssd_buf]
        BT = [view(r, 3328, 2, P) for r in ssd_buf]
        EC = [view(r, 3584, 4, P) for r in ssd_buf]
        acc = view(reg_t, 0, 4, P)
        xsd = [view(reg_t, 512, 4, P), view(reg_t, 1024, 4, P)]
        ST = [view(reg_t, 1536, HEADS * HD), view(reg_t, 2048, HEADS * HD)]
        st_io = view(reg_t, 2560, 4, P)
        st_out = [view(reg_t, 3072, 4, P), view(reg_t, 3584, 4, P)]
        sq = view(reg_u, 2048, 4, T)
        mnT = view(reg_u, 0, KD, MEM)
        k_tok = view(act_a, 2560, 2, D)
        kT = [view(reg_g, 0, KD, MEM), view(conv, 0, KD, MEM)]
        v_tok = [view(reg_g, 2048, 2, D), view(conv, 2048, 2, D)]
        ks_rows = view(reg_t, 0, 2, D)
        PR = [view(reg_r, 512 * i, 2, MEM) for i in range(2)]
        PT = [view(reg_r, 1024 + 512 * i, 4, P) for i in range(2)]
        H = view(reg_u, 0, NT, D)
        xg = [view(reg_r, 1024 * i, D) for i in range(2)]
        yo = [view(reg_r, 2048 + 1024 * i, D) for i in range(2)]
        xgT = [view(reg_t, 640 * i, KD, CAP) for i in range(2)]
        gact = [view(reg_t, 1280 + 160 * i, 2, CAP) for i in range(2)]
        hid = [view(reg_t, 1600 + 160 * i, 2, CAP) for i in range(2)]
        rt_off = [0]

        def rt(*shape):
            n = 1
            for s in shape:
                n *= s
            v = view(conv, rt_off[0], *shape)
            rt_off[0] += n
            return v

        lg = rt(NT, NG + NE)
        lgT = rt(T)
        r_gm, r_gs, r_gp, r_m1, r_m2, r_d, r_e, r_k1, r_k2 = [rt(NT, 1) for _ in range(9)]
        r_gl, r_pr, r_go = [rt(NT, NG) for _ in range(3)]
        r_sel, r_eq, r_e1, r_e2, r_es = [rt(NT, EG) for _ in range(5)]
        r_full = rt(NT, NE)
        ind1, ind2 = [rt(NT, NE) for _ in range(2)]
        ind, before = [rt(NT + 1, NE) for _ in range(2)]
        oh = [rt(NT, CAP) for _ in range(2)]
        mv = [rt(NT, NE) for _ in range(2)]
        idx_f = rt(2, NE)
        r_max = rt(1)
        prio = rt(EG)
        tok_id = rt(NT)
        slot_id = rt(CAP)
        gates = sb("gates", [P, 2, NT])
        iot = sb("iota_int", [P, CAP + NT + EG], I32)
        flag = sb("overflow_flag", [P, 1], I32)
        idx_y = sb("scatter_index", [P, NE], I32)
        idx_x = sb("gather_index", [P, NE], I32)
        cur_x = sb("gather_now", [P, 2], I32)
        cur_y = sb("scatter_now", [P, 2], I32)
        y2 = [view(reg, off, 2, D) for reg, off in ((reg_g, 0), (reg_g, 2048), (act_a, 0), (act_a, 2048), (act_b, 0))]

        banks = [ctx.enter_context(nc.psum_tensor(f"bank{i}", [P, 512], F32)) for i in range(8)]

        filled = sem("psum_filled")
        emptied = {"act": sem("emptied_by_act"), "dve": sem("emptied_by_dve")}
        ring_loaded = [sem(f"ring_loaded{i}") for i in range(SLOTS)]
        par_loaded = sem("s5_params_loaded")
        more_loaded = [sem(f"more_loaded{i}") for i in range(6)]
        row_loaded = [sem(f"row_loaded{i}") for i in range(3)]
        s5_loaded, vec_loaded, small_loaded = sem("s5_loaded"), sem("vec_loaded"), sem("small_loaded")
        gain_loaded = [sem("gain_loaded0"), sem("gain_loaded1")]
        route_loaded = sem("router_weights_loaded")
        ident_ready, consts = sem("identity_ready"), sem("consts_ready")
        dstep, pstep = sem("dve_step"), sem("pool_step")
        ms_ready, rstd_ready, normed = sem("ms_ready"), sem("rstd_ready"), sem("rows_normed")
        small_done = sem("act_small_done")
        small_ask = sem("dve_small_asked")
        lam_ready, R_ready, G_ready = [sem(n) for n in ("lam_ready", "R_ready", "G_ready")]
        bd_ready, h_ready = sem("bd_ready"), sem("s5_states_ready")
        tap_ready, T_zero, T_ready = sem("tap_ready"), sem("T_zeroed"), sem("T_loaded")
        conv_pad, conv_first, conv_sum, conv_done = [sem(n) for n in
            ("conv_pads_ready", "conv_first_tap", "conv_summed", "conv_done")]
        da_ready, du_ready, mm_ready, xde_ready, xsd_ready = [sem(n) for n in
            ("da_ready", "du_ready", "mm_ready", "xde_ready", "xsd_ready")]
        st_loaded, st_ready, y_gated, squared, sn_ready = [sem(n) for n in
            ("state_loaded", "state_updated", "y_gated", "y_squared", "ssd_normed")]
        mix_done = sem("mix_done")
        mix_stored, st_stored, kv_stored = sem("mixer_rows_stored"), sem("ssd_states_stored"), sem("memory_kv_stored")
        wdt_loaded = sem("wdt_loaded")
        h_loaded, attn_loaded, ks_loaded = sem("h_loaded"), sem("sample_v_loaded"), sem("sample_k_loaded")
        mx_ready, pn_ready = [sem(n) for n in ("max_ready", "probs_normed")]
        f_stored = [sem(f"ffn_rows_stored{i}") for i in range(3)]
        y2_loaded = [sem(f"y2_loaded{t}") for t in range(NT)]
        y2_added, h_final, h_squared, y_scaled, y_normed = [sem(n) for n in
            ("y2_added", "h_final", "h_squared", "y_scaled", "y_rows_by_dve")]
        y_stored = [sem(f"y_stored{i}") for i in range(3)]
        iota_ready, route_ask, route_done, ind_ready = [sem(n) for n in
            ("iota_ready", "route_exp_asked", "route_exp_done", "indicators_ready")]
        table_step, oh_ready, slots_filled, idx_ready, pass_done = [sem(n) for n in
            ("table_step", "slot_onehots_ready", "slots_filled", "indices_ready", "pass_scattered")]
        gx_copied, gy_copied = sem("gather_index_copied"), sem("scatter_index_copied")
        gathered, scattered = [sem("gathered0"), sem("gathered1")], [sem("scattered0"), sem("scattered1")]
        turned_x = sem("xg_turned")
        xT_act, xT_dve = sem("xgT_by_act"), sem("xgT_by_dve")
        gate_done, gu_done, silu_done, hid_ready = sem("gate_done"), sem("gate_up_done"), sem("silu_done"), sem("hidden_ready")
        dn_done = sem("down_done")
        yo_act, yo_dve = sem("rows_by_act"), sem("rows_by_dve")
        waits_done = sem("pool_waits_done")
        xg_zero, experts_done = sem("gather_buffers_zeroed"), sem("experts_done")

        def norm_len(n):
            return staged[n][1] if n < NORM_H else TOK[(n - NORM_H) % NT][1]

        def bank_of(*key):
            return banks[job[key] % 8]

        def wait_filled(eng, *key):
            eng.wait_ge(filled, job[key] + 1)
            return bank_of(*key)

        def wait_emptied(eng, *key):
            who, n = rank[job[key]]
            eng.wait_ge(emptied[who], n)

        chunks = []
        for c in range(2):
            chunks.append(dram("w_in", "o (k p) n -> p (o k) n", p=P)[:, :, COL_U + CW * c:COL_U + CW * (c + 1)])
        for col in [COL_Z] + [COL_XBC + CW * c for c in range(4)] + [COL_Z + CW]:
            chunks.append(dram("w_in", "o (k p) n -> p (o k) n", p=P)[:, :, col:col + CW])
        chunks.append(dram("s5_w_glu", "o (k p) (c n) -> p (o k) c n", p=P, n=CW))
        for name in ("w_v", "w_k", "w_out", "w_q", "w_o"):
            for c in range(4):
                chunks.append(dram(name, "o (k p) n -> p (o k) n", p=P)[:, :, CW * c:CW * (c + 1)])
        chunk_end = ([("u", 2 * c + 1, 1) for c in range(2)] + [("z", 1, 1)]
                     + [("xbc", 2 * c + 1, 1) for c in range(4)] + [("z", 3, 1), ("glu", 3, 1)]
                     + [(w, c, 1) for w in ("v_mem", "k_mem") for c in range(4)]
                     + [("out", NT - 1, c // 2) for c in range(4)] + [("q", 2 * c + 1, 1) for c in range(4)]
                     + [("o", NT - 1, c // 2) for c in range(4)])
        CH_U, CH_Z, CH_XBC, CH_GLU, CH_KV, CH_OUT, CH_Q, CH_O = 0, (2, 7), 3, 8, 9, 17, 21, 25
        NCH = len(chunks)
        assert NCH == CH_O + 4

        def slot(c):
            return ring[:, c % SLOTS, :, :]

        def wait_chunk(eng, c):
            eng.wait_ge(ring_loaded[c % SLOTS], 16 * (c // SLOTS + 1))

        x_rows = [a["x_prompt"][0, t0:t0 + n, :] if t < 4 else a["x_sample"][0, :, :] for t, (t0, n) in enumerate(TOK)]
        mem_rows = [a["mem_prompt"][0, P * t:P * (t + 1), :] for t in range(2)]
        staged = [(x_rows[t], TOK[t][1]) for t in range(NT)] + [(mem_rows[t], P) for t in range(2)]
        NORM_X, NORM_M, NORM_H, NORM_F, NORM_Y = 0, 5, 7, 12, 17
        ROW_SLOT = [0, 1, 2, 0, 1, 0, 1]
        ROW_TURN = [1, 1, 1, 2, 2, 3, 3]

        LAST = NE // 2 - 1
        ring_k = [ring[:, k, :, :].rearrange("p k n -> p (k n)") for k in range(SLOTS)]
        g0, g1 = view(reg_g, 0, 2048), view(reg_g, 2048, 2048)
        a0, a1 = view(act_a, 0, 2048), view(act_a, 2048, 2048)
        b0, b1 = view(act_b, 0, 2048), view(act_b, 2048, 2048)
        WSET = [ring_k[0:3], ring_k[3:6], [g0, g1, a0], [a1, b0, b1]]
        WSEM = [ring_loaded[0:3], ring_loaded[3:6], more_loaded[0:3], more_loaded[3:6]]
        SETS = len(WSET)
        QUADS = NE // SETS
        WFREE = ([chunk_end[max(c for c in range(NCH) if c % SLOTS == k)] for k in range(SLOTS)]
                 + [("pv", 2 * NT - 1)] * 2 + [("routef", 2)] * 2 + [("o", NT - 1, 1)] * 2)
        WDENSE = [len(range(i, NCH, SLOTS)) for i in range(SLOTS)] + [0] * 6
        experts_of = [a["w_gate"].rearrange("o e (p k) f -> (o e) p (k f)", p=P),
                      a["w_up"].rearrange("o e (p k) f -> (o e) p (k f)", p=P),
                      a["w_down"].rearrange("o e (p m) d -> (o e) p (m d)", p=P)]

        def wait_expert_chunk(eng, part, qq, s):
            eng.wait_ge(WSEM[s][part], 16 * qq + 16 * (WDENSE[3 * s + part] + 1))

        def overflow_passes(eng, run_pass):
            eng.wait_ge(idx_ready, 1)
            over = eng.value_load(flag[0:1, 0:1], min_val=0, max_val=1)
            with eng.If(over > 0):
                with eng.Fori(1, PASSES) as p:
                    run_pass(p)

        PAR_LOADS, S5_LOADS, VEC_LOADS, SMALL_LOADS = 6, 6, 5, 3
        block = ctx.enter_context(nc.Block())


        @block.sync
        def _(sp):
            def load_rows(n):
                sp.dma_start(rows[0:staged[n][1], ROW_SLOT[n], :], staged[n][0]).then_inc(row_loaded[ROW_SLOT[n]], 16)

            def load_chunk(c):
                if c >= SLOTS:
                    wait_filled(sp, *chunk_end[c - SLOTS])
                dst = slot(c).rearrange("p (k c) n -> p k (c n)", c=2) if c == CH_GLU else slot(c)
                sp.dma_start(dst, chunks[c]).then_inc(ring_loaded[c % SLOTS], 16)

            def load_gain(g, name):
                src = a[name] if name == "norm_final" else a[name].rearrange("o d -> (o d)")
                sp.dma_start(gain[:, g, :], src.partition_broadcast(P)).then_inc(gain_loaded[g], 16)

            load_rows(0)
            load_gain(0, "norm_mix")
            load_rows(1)
            load_rows(2)
            sp.dma_start(vec_rows[0:4, :], a["conv_w"].rearrange("o k c -> (o k) c")).then_inc(vec_loaded, 16)
            sp.dma_start(vec_rows[4:5, :], a["conv_b"]).then_inc(vec_loaded, 16)
            for copy in range(2):
                sp.dma_start(vec_rows[5:6, SSD_W * copy:SSD_W * (copy + 1)], a["ssd_norm"]).then_inc(vec_loaded, 16)
            sp.dma_start(vec_rows[6:9, :], a["cache_conv"].rearrange("o b k c -> (o b k) c")).then_inc(vec_loaded, 16)
            load_chunk(0)
            for n in (3, 4):
                wait_filled(sp, "xT", n - 3, 1)
                load_rows(n)
            load_chunk(1)
            sp.dma_start(w_dt[:, :, :], dram("w_in", "o (k p) n -> p (o k) n", p=P)[:, :, COL_DT:COL_DT + HEADS])\
                .then_inc(wdt_loaded, 16)
            sp.dma_start(dt_b[:, :], a["dt_bias"].rearrange("o h -> (o h)").partition_broadcast(P)).then_inc(small_loaded, 16)
            sp.dma_start(a_lg[:, :], a["a_log"].rearrange("o h -> (o h)").partition_broadcast(P)).then_inc(small_loaded, 16)
            sp.dma_start(dsk_rows[:, :], a["d_skip"].rearrange("o h -> (o h)").partition_broadcast(P))\
              .then_inc(small_loaded, 16)
            load_gain(1, "norm_mem")
            for c in range(2, CH_GLU):
                load_chunk(c)
            sp.dma_start(w_rt[:, :, 0:NG], dram("w_router_group", "o (k p) n -> p (o k) n", p=P)).then_inc(route_loaded, 16)
            sp.dma_start(w_rt[:, :, NG:], a["w_router_expert"].rearrange("o d g e -> (o d) (g e)")
                         .rearrange("(k p) n -> p k n", p=P)).then_inc(route_loaded, 16)
            sp.dma_start(b_rt[:, 0:NG], a["b_router_group"].rearrange("o g -> (o g)").partition_broadcast(P))\
              .then_inc(route_loaded, 16)
            sp.dma_start(b_rt[:, NG:], a["b_router_expert"].rearrange("o g e -> (o g e)").partition_broadcast(P))\
              .then_inc(route_loaded, 16)
            sp.wait_ge(tap_ready, 1)
            sp.wait_ge(T_zero, 1)
            for k in range(8):
                s = 7 - k
                for g2 in range(2):
                    sp.dma_start(Tm[GC * k:GC * (k + 1), g2::2, GC * s:P],
                                 tap[GC * g2:GC * (g2 + 1), :, 0:P - GC * s]).then_inc(T_ready, 16)
            for c in range(CH_GLU, CH_GLU + SLOTS):
                if c == CH_GLU + 4:
                    sp.wait_ge(h_ready, 1)
                    load_rows(5)
                    load_rows(6)
                load_chunk(c)
            sp.wait_ge(filled, job[("y", 3, 1)] + 1)
            sp.dma_start(st_io, a["state_ssd"].rearrange("a b h p n -> (a b h p) n")
                         .rearrange("(i q) n -> q i n", q=P)).then_inc(st_loaded, 16)
            load_chunk(CH_GLU + SLOTS)
            sp.wait_ge(normed, 7)
            load_gain(0, "norm_x")
            load_gain(1, "norm_ffn")
            for c in range(CH_GLU + SLOTS + 1, CH_OUT + 1):
                load_chunk(c)
            wait_filled(sp, "ssq")
            sp.dma_start(v_tok[1], a["cache_mem_v"].rearrange("a b m h d -> (a b m) (h d)")
                         .rearrange("(t q) n -> q t n", q=P)).then_inc(attn_loaded, 16)
            sp.dma_start(ks_rows, a["cache_mem_k"].rearrange("a b m h d -> (a b m) (h d)")
                         .rearrange("(t q) n -> q t n", q=P)).then_inc(ks_loaded, 16)
            sp.wait_ge(mix_stored, 16 * (4 + 2))

            def load_h(t):
                sp.dma_start(H[0:TOK[t][1], t, :], x_rows[t]).then_inc(h_loaded, 16)

            for t in (2, 3, 4):
                load_h(t)
            for c in range(CH_OUT + 1, CH_Q):
                load_chunk(c)
            wait_filled(sp, "k_mem", 3, 1)
            for t in (0, 1):
                load_h(t)
            for c in range(CH_Q, NCH):
                load_chunk(c)

            def load_part(qq, i, s, part):
                if isinstance(qq, int) and qq == 0:
                    wait_filled(sp, *WFREE[3 * s + part])
                    if s == 2:
                        sp.wait_ge(kv_stored, 32)
                elif part < 2:
                    sp.wait_ge(gu_done, 4 * qq + (s - 3))
                else:
                    sp.wait_ge(dn_done, 8 * qq + (2 * s - 6))
                sp.dma_start(WSET[s][part], experts_of[part][bass.ds(SETS * i + s, 1), :, :]
                             .rearrange("e p n -> p (e n)")).then_inc(WSEM[s][part], 16)

            def sp_pass(p):
                first = p * QUADS
                order = [(0, 0), (1, 2), (2, 0), (2, 1), (0, 1), (0, 2), (1, 0), (1, 1), (2, 2), (3, 0), (3, 1), (3, 2)]
                for s, part in (order if isinstance(p, int) else sorted(order)):
                    load_part(first, 0, s, part)
                with sp.Fori(1, QUADS) as i:
                    for s in range(SETS):
                        for part in range(3):
                            load_part(first + i, i, s, part)

            sp_pass(0)
            sp.wait_ge(normed, NORM_H + NT)
            load_gain(0, "norm_final")
            overflow_passes(sp, sp_pass)

            sp.wait_ge(experts_done, 1)
            for t, (t0, L) in enumerate(TOK):
                sp.dma_start(y2[t][0:L], y2_dram[2 * t0:2 * (t0 + L), :].rearrange("(t k) d -> t k d", k=2))\
                    .then_inc(y2_loaded[t], 16)
            for t, (t0, L) in enumerate(TOK):
                if t < Y_POOL:
                    sp.wait_ge(normed, NORM_Y + t + 1)
                    src = rows[0:L, t, :]
                else:
                    sp.wait_ge(y_normed, t - Y_POOL + 1)
                    src = y2[t][0:L, 1, :]
                dst = o["y_prompt"][0, t0:t0 + L, :] if t < 4 else o["y_sample"][0, :, :]
                sp.dma_start(dst, src).then_inc(y_stored[t % 3], 16)
            for i in range(3):
                sp.wait_ge(y_stored[i], 16 * len(range(i, NT, 3)))
            sp.wait_ge(st_stored, 32)
            sp.wait_ge(mix_stored, 16 * 6)

        @block.gpsimd
        def _(pool):
            n = [0]

            def step(ins):
                n[0] += 1
                return ins.then_inc(pstep, 1)

            def sync():
                pool.wait_ge(pstep, n[0])

            step(pool.memset(ident[:, :], 0.0))
            sync()
            pool.affine_select(out=ident[:, :], in_=ident[:, :], compare_op=ALU.not_equal, fill=1.0,
                               base=0, pattern=[[-1, P]], channel_multiplier=1).then_inc(ident_ready, 1)
            for m in (tri_le, tri_gt, tri_lt, ones):
                step(pool.memset(m[:, :], 1.0))
            sync()
            step(pool.affine_select(out=tri_le[:, :], in_=tri_le[:, :], compare_op=ALU.is_ge, fill=0.0,
                                    base=0, pattern=[[1, P]], channel_multiplier=-1))
            step(pool.affine_select(out=tri_gt[:, :], in_=tri_gt[:, :], compare_op=ALU.is_gt, fill=0.0,
                                    base=0, pattern=[[-1, P]], channel_multiplier=1))
            step(pool.affine_select(out=tri_lt[:, :], in_=tri_lt[:, :], compare_op=ALU.is_gt, fill=0.0,
                                    base=0, pattern=[[1, P]], channel_multiplier=-1))
            pool.wait_ge(par_loaded, 16 * PAR_LOADS)
            step(pool.tensor_copy(p_rows[0:16, 2, :].rearrange("q (g n) -> q g n", g=2),
                                  ld_rows[0:16, :].unsqueeze(2).to_broadcast([16, 2, SN])))
            sync()
            pool.memset(bd, 0.0).then_inc(consts, 1)

            wait_emptied(pool, "cT", 0)
            wait_emptied(pool, "cT", 1)
            pool.wait_ge(lam_ready, 1)
            pa = prod_a.rearrange("p (q k c) -> p q k c", q=PAIRS, k=9)

            def over_c(v):
                return v[:, :, :].rearrange("p k q -> p q k").unsqueeze(3).to_broadcast([P, PAIRS, 9, GC])

            def over_k(v):
                return v.unsqueeze(2).to_broadcast([P, PAIRS, 9, GC])

            for part, (c1, p1, c2, p2) in enumerate(((0, powr, 2, powi), (1, powi, 2, powr))):
                g = G[:, part].rearrange("p q (k c) -> p q k c", k=9)
                step(pool.tensor_tensor(g, over_k(c_t[:, c1]), over_c(p1), ALU.mult))
                step(pool.tensor_tensor(pa, over_k(c_t[:, c2]), over_c(p2), ALU.mult))
                sync()
                step(pool.tensor_tensor(g, g, pa, ALU.add))
                sync()
            pool.tensor_copy(s5s[:, 19, :], s5p[:, 3, :]).then_inc(G_ready, 1)

            wait_filled(pool, "tap", 3)
            pool.wait_ge(R_ready, 1)
            step(pool.memset(xbc[:, :, 0:3], 0.0))
            wait_emptied(pool, "vec")
            sync()
            pool.tensor_copy(xbc[:, :, NP + 3:NP + 6], vecT[:, :, 6:9]).then_inc(conv_pad, 1)
            wait_filled(pool, "v", 7)
            pool.memset(Tm, 0.0).then_inc(T_zero, 1)

            for c, (t0, L) in enumerate(TOK):
                b = c % 2
                if c == 0:
                    wait_filled(pool, "glu", 3, 1)
                    pool.wait_ge(da_ready, 1)
                if c >= 2:
                    wait_filled(pool, "seg", c - 2, 1)
                pool.tensor_tensor(DU[b][0:L, :, 0:L], da_v[0:L, c, :].unsqueeze(2).to_broadcast([L, HEADS, L]),
                                   tri_le[0:L, 0:L].unsqueeze(1).to_broadcast([L, HEADS, L]), ALU.mult)\
                    .then_inc(du_ready, 1)
                if c >= 2:
                    pool.wait_ge(y_gated, c - 1)
                pool.tensor_tensor(xsd[b][:, :, 0:L], xbc[:, 0:4, XC[c]:XC[c] + L],
                                   dsk[:, :].unsqueeze(2).to_broadcast([P, 4, L]), ALU.mult).then_inc(xsd_ready, 1)
                wait_emptied(pool, "xs", c)
                wait_emptied(pool, "tot", c)
                if c >= 2:
                    wait_filled(pool, "state", c - 2)
                pool.tensor_tensor(XDE[b][0:L], XDT[b][0:L],
                                   expo[0:L, b, 0:HEADS].unsqueeze(2).to_broadcast([L, HEADS, HD]), ALU.mult)\
                    .then_inc(xde_ready, 1)

            step(pool.iota(iot[:, 0:CAP], [[1, CAP]], base=0, channel_multiplier=0))
            step(pool.iota(iot[:, CAP:CAP + NT], [[2 * P, NT]], base=1, channel_multiplier=2))
            pool.iota(iot[:, CAP + NT:], [[-1, EG]], base=EG, channel_multiplier=0).then_inc(iota_ready, 1)
            wait_filled(pool, "pv", 2 * NT - 1)
            for b in range(2):
                pool.memset(xg[b][0:CAP], 0.0).then_inc(xg_zero, 1)
            pool.wait_ge(xg_zero, 2)
            for i in range(3):
                pool.wait_ge(f_stored[i], 16 * len(range(i, NT, 3)))

            def gather(pp, i, b, reused=True):
                if reused:
                    pool.wait_ge(turned_x, 4 * pp + (2 * b - 2))
                    pool.sem_inc(waits_done, 1)
                pool.tensor_copy(cur_x[0:CAP, b:b + 1], idx_x[0:CAP, bass.ds(2 * i + b, 1)]).then_inc(gx_copied, 1)
                pool.wait_ge(gx_copied, 2 * pp + (b + 1))
                pool.sem_inc(waits_done, 1)
                pool.indirect_dma_start(
                    out=xg[b][0:CAP], out_offset=None, in_=xf_dram[:, :],
                    in_offset=bass.IndirectOffsetOnAxis(ap=cur_x[0:CAP, b:b + 1], axis=0),
                    bounds_check=T - 1, oob_is_err=False).then_inc(gathered[b], 16)

            def scatter(pp, i, b, reused=True):
                if reused:
                    pool.wait_ge(scattered[b], 16 * pp)
                    pool.sem_inc(waits_done, 1)
                pool.tensor_copy(cur_y[0:CAP, b:b + 1], idx_y[0:CAP, bass.ds(2 * i + b, 1)]).then_inc(gy_copied, 1)
                pool.wait_ge(gy_copied, 2 * pp + (b + 1))
                pool.wait_ge(yo_act, 2 * pp + (b + 1))
                pool.wait_ge(yo_dve, 2 * pp + (b + 1))
                pool.sem_inc(waits_done, 1)
                pool.indirect_dma_start(
                    out=y2_dram[:, :], out_offset=bass.IndirectOffsetOnAxis(ap=cur_y[0:CAP, b:b + 1], axis=0),
                    in_=yo[b][0:CAP], in_offset=None,
                    bounds_check=2 * T - 1, oob_is_err=False).then_inc(scattered[b], 16)

            def pool_pass(p):
                first = p * (LAST + 1)
                again = not isinstance(p, int)
                pool.wait_ge(idx_ready, p + 1)
                pool.sem_inc(waits_done, 1)
                for b in range(2):
                    gather(first, 0, b, reused=again)
                for b in range(2):
                    gather(first + 1, 1, b)
                    scatter(first, 0, b, reused=again)
                with pool.Fori(1, LAST) as i:
                    for b in range(2):
                        gather(first + i + 1, i + 1, b)
                        scatter(first + i, i, b)
                for b in range(2):
                    scatter(first + LAST, LAST, b)
                for b in range(2):
                    pool.wait_ge(scattered[b], 16 * (first + LAST + 1))
                pool.sem_inc(pass_done, 1)

            pool_pass(0)
            overflow_passes(pool, pool_pass)
            pool.sem_inc(experts_done, 1)
            pool.wait_ge(gain_loaded[0], 48)
            for t, (t0, L) in enumerate(TOK[0:Y_POOL]):
                pool.wait_ge(y_scaled, t + 1)
                pool.tensor_tensor(rows[0:L, t % 3, :], rows[0:L, t % 3, :], gain[0:L, 0, :], ALU.mult)\
                    .then_inc(normed, 1)

        @block.tensor
        def _(pe):
            def claim(*key):
                j = job[key]
                if j >= 8:
                    who, m = rank[j - 8]
                    pe.wait_ge(emptied[who], m)
                return banks[j % 8]

            def turn(out, in_):
                m = in_.shape[0]
                return pe.transpose(out, in_, ident[0:m, 0:m])

            def turn_rows(stage, t, first, L):
                for h in range(2):
                    ps = claim(stage, t, h)
                    if h == 0:
                        pe.wait_ge(normed, first + t + 1)
                    for k in range(4):
                        kk = 4 * h + k
                        s = ROW_SLOT[first + t] if first < NORM_H else t % 3
                        m = turn(ps[:, P * k:P * k + L], rows[0:L, s, P * kk:P * (kk + 1)])
                    m.then_inc(filled, 1)

            pe.wait_ge(ident_ready, 1)
            turn_rows("xT", 0, NORM_X, P)
            turn_rows("xT", 1, NORM_X, P)
            pe.wait_ge(consts, 1)
            pe.wait_ge(vec_loaded, 16 * VEC_LOADS)
            ps = claim("vec")
            for k in range(8):
                m = turn(ps[:, 9 * k:9 * k + 9], vec_rows[0:9, P * k:P * (k + 1)])
            m.then_inc(filled, 1)
            pe.wait_ge(par_loaded, 16 * PAR_LOADS)
            ps = claim("s5par")
            for k in range(5):
                turn(ps[:, 16 * k:16 * k + 16], p_rows[0:16, k, :])
            m = turn(ps[0:2 * GC, 80:96], s5d_rows[0:16, :])
            m.then_inc(filled, 1)
            turn_rows("xT", 2, NORM_X, P)
            def project_half(stage, c, mt, h, x):
                ps = claim(stage, mt, h)
                for k in range(KD):
                    m = pe.matmul(ps[:, 0:HALF], slot(c)[:, k, P * (mt % 2):P * (mt % 2 + 1)],
                                  x[:, k, HALF * h:HALF * (h + 1)], start=(k == 0), stop=(k == KD - 1))
                m.then_inc(filled, 1)

            def project(stage, first_chunk, m0, m1, x):
                for mt in range(m0, m1):
                    c = first_chunk + mt // 2
                    wait_chunk(pe, c)
                    for h in range(2):
                        project_half(stage, c, mt, h, x)

            def project_z(mt, h):
                wait_chunk(pe, CH_Z[mt // 2])
                project_half("z", CH_Z[mt // 2], mt, h, xT)

            def project_u(h, m0, m1):
                wait_emptied(pe, "xT", 2 + 2 * h, 1)
                for mt in range(m0, m1):
                    wait_chunk(pe, CH_U + mt // 2)
                    project_half("u", CH_U + mt // 2, mt, h, xT)

            project_u(0, 0, 1)
            for ri in range(2):
                ps = claim("cT", ri)
                pe.wait_ge(s5_loaded, 16 * S5_LOADS)
                for i in range(4):
                    m = turn(ps[:, P * i:P * (i + 1)], c_rows[:, ri, i].rearrange("p a n -> p (a n)"))
                m.then_inc(filled, 1)
            project_u(0, 1, 2)
            turn_rows("xT", 3, NORM_X, P)
            turn_rows("xT", 4, NORM_X, NS)
            project_u(0, 2, 4)
            project_u(1, 0, 4)
            for b in range(8):
                ps = claim("wT", b)
                if b == 0:
                    pe.wait_ge(R_ready, 1)
                for i in range(4):
                    q, ri = 2 * b + i // 2, i % 2
                    m = turn(ps[:, P * i:P * (i + 1)], R[:, ri, q].rearrange("p k c -> p (k c)"))
                m.then_inc(filled, 1)
            for i in range(4):
                for h in range(2):
                    ps = claim("uj", i, h)
                    wait_emptied(pe, "u", i, 1)
                    for k in range(4 * h, 4 * h + 4):
                        m = turn(ps[0:NJ, P * (k % 4):P * (k % 4 + 1)], uT[:, i, 7 - k::Q8])
                    m.then_inc(filled, 1)
                project_z(i // 2, i % 2)
                for h in range(2):
                    ps = claim("ug", i, h)
                    wait_emptied(pe, "uj", i, 1)
                    for g in range(4 * h, 4 * h + 4):
                        m = turn(ps[:, NJ * (g % 4):NJ * (g % 4 + 1)], Uj[0:NJ, i % 2, g, :])
                    m.then_inc(filled, 1)
            for b in range(8):
                ps = claim("v", b)
                wait_emptied(pe, "wT", b)
                wait_emptied(pe, "ug", b // 2, b % 2)
                for qq in range(2):
                    q = 2 * b + qq
                    for ri in range(2):
                        for g2 in range(2):
                            off = (2 * qq + ri) * NJ
                            m = pe.matmul(ps[SN * g2:SN * (g2 + 1), off:off + NJ],
                                          WT[:, q, ri, SN * g2:SN * (g2 + 1)], U[:, 2 * q + g2, :],
                                          start=True, stop=True)
                m.then_inc(filled, 1)
            for b in range(4):
                ps = claim("tap", b)
                if b == 0:
                    pe.wait_ge(G_ready, 1)
                    pe.wait_ge(bd_ready, 4)
                for i in range(4):
                    q = 4 * b + i
                    for ri in range(2):
                        m = pe.matmul(ps[0:32, P * i:P * (i + 1)], bd[:, ri, q, :], G[:, ri, q, 0:P],
                                      start=(ri == 0), stop=(ri == 1))
                m.then_inc(filled, 1)
            pe.wait_ge(wdt_loaded, 16)
            for h in range(2):
                ps = claim("dtf", h)
                for k in range(KD):
                    m = pe.matmul(ps[0:HEADS, 0:HALF], w_dt[:, k, :], xT[:, k, HALF * h:HALF * (h + 1)],
                                  start=(k == 0), stop=(k == KD - 1))
                m.then_inc(filled, 1)
            ps = claim("dt")
            wait_emptied(pe, "dtf", 1)
            for t, (t0, L) in enumerate(TOK):
                m = turn(ps[0:L, 8 * t:8 * t + 8], dtT[:, t0:t0 + L])
            m.then_inc(filled, 1)
            project("xbc", CH_XBC, 0, 8, xT)
            for mt in range(2, 4):
                for h in range(2):
                    project_z(mt, h)
            for i in range(4):
                for g2 in range(2):
                    ps = claim("y", i, g2)
                    if i == 0 and g2 == 0:
                        pe.wait_ge(h_ready, 1)
                        pe.wait_ge(T_ready, 16 * 16)
                    for qq in range(4):
                        q = 4 * i + qq
                        g = 2 * q + g2
                        out = ps[0:NJ, P * qq:P * (qq + 1)]
                        half = slice(SN * g2, SN * (g2 + 1))
                        pe.matmul(out, U[:, g, :], Tm[:, g, :], start=True, stop=False)
                        pe.matmul(out, SS[half, q, 0:NJ], G[half, 0, q, GC:9 * GC], start=False, stop=False)
                        m = pe.matmul(out, SS[half, PAIRS + q, 0:NJ], G[half, 1, q, GC:9 * GC],
                                      start=False, stop=True)
                    m.then_inc(filled, 1)
                for h in range(2):
                    ps = claim("yT", i, h)
                    wait_emptied(pe, "y", i, 1)
                    for s in range(4):
                        m = turn(ps[:, NJ * s:NJ * (s + 1)], Yj[0:NJ, i % 2, 4 * h + s, :])
                    m.then_inc(filled, 1)
            wait_chunk(pe, CH_GLU)
            for mt in range(4):
                for h in range(2):
                    ps = claim("glu", mt, h)
                    if mt == 0:
                        wait_emptied(pe, "yT", 3, 1)
                    for k in range(4):
                        m = pe.matmul(ps[:, 0:HALF], slot(CH_GLU)[:, 2 * k + mt // 2, P * (mt % 2):P * (mt % 2 + 1)],
                                      mix[:, 4 + k, HALF * h:HALF * (h + 1)], start=(k == 0), stop=(k == 3))
                    m.then_inc(filled, 1)
            ps = claim("s5fin")
            for k in range(4):
                m = turn(ps[0:16, P * k:P * (k + 1)], s5f[:, k, :])
            m.then_inc(filled, 1)
            for b in range(2):
                for h in range(2):
                    ps = claim("convT", b, h)
                    for k in range(4):
                        x0 = (NP, CONV_OUT)[b]
                        m = turn(ps[0:3, P * k:P * (k + 1)], xbc[:, 4 * h + k, x0:x0 + 3])
                    m.then_inc(filled, 1)
            ps = claim("stin")
            pe.wait_ge(st_loaded, 16)
            for i in range(4):
                m = turn(ps[:, P * i:P * (i + 1)], st_io[:, i, :])
            m.then_inc(filled, 1)

            def prep(c):
                t0, L = TOK[c]
                b, x0 = c % 2, XC[c]
                ps = claim("tot", c)
                if c == 0:
                    pe.wait_ge(da_ready, 1)
                pe.matmul(ps[0:L, 0:8], tri_gt[0:L, 0:L], da_v[0:L, c, :], start=True, stop=True)
                pe.matmul(ps[:, 8:16], ones[0:L, :], da_v[0:L, c, :], start=True, stop=True).then_inc(filled, 1)
                ps = claim("cs", c)
                for h in range(HEADS):
                    m = pe.matmul(ps[HD * (h % 2):HD * (h % 2 + 1), L * (h // 2):L * (h // 2 + 1)],
                                  da_v[0:L, c, h:h + 1].to_broadcast([L, HD]),
                                  tri_le[0:L, 0:L], start=True, stop=True)
                m.then_inc(filled, 1)
                for hg in range(2):
                    ps = claim("seg", c, hg)
                    pe.wait_ge(du_ready, c + 1)
                    pe.matmul(ps[0:L, 0:4 * L], tri_gt[0:L, 0:L], DU[b][0:L, 4 * hg:4 * hg + 4, 0:L],
                              start=True, stop=True).then_inc(filled, 1)
                ps = claim("cb", c)
                if c == 0:
                    pe.wait_ge(conv_done, 8)
                for g in range(2):
                    m = pe.matmul(ps[0:L, L * g:L * (g + 1)], xbc[:, 4 + g, x0:x0 + L], xbc[:, 6 + g, x0:x0 + L],
                                  start=True, stop=True)
                m.then_inc(filled, 1)
                ps = claim("xs", c)
                for i in range(4):
                    m = turn(ps[0:L, P * i:P * (i + 1)], xbc[:, i, x0:x0 + L])
                m.then_inc(filled, 1)
                ps = claim("bt", c)
                for g in range(2):
                    m = turn(ps[0:L, P * g:P * (g + 1)], xbc[:, 4 + g, x0:x0 + L])
                m.then_inc(filled, 1)

            def memory(stage, first_chunk, c):
                wait_chunk(pe, first_chunk + c)
                wait_emptied(pe, "memT", 1, 1)
                for t in range(2):
                    ps = claim(stage, c, t)
                    for k in range(KD):
                        m = pe.matmul(ps[:, 0:CW], mnT[:, k, P * t:P * (t + 1)], slot(first_chunk + c)[:, k, :],
                                      start=(k == 0), stop=(k == KD - 1))
                    m.then_inc(filled, 1)

            prep(0)
            for t in range(2):
                turn_rows("memT", t, NORM_M, P)
            for c, (t0, L) in enumerate(TOK):
                if c + 1 < NT:
                    prep(c + 1)
                b, x0, st = c % 2, XC[c], ST[c // 4]
                ps = claim("yoff", c)
                if c == 0:
                    pe.wait_ge(st_ready, 1)
                else:
                    wait_emptied(pe, "state", c - 1)
                for i in range(4):
                    m = pe.matmul(ps[:, L * i:L * (i + 1)], st[:, P * i:P * (i + 1)], xbc[:, 6 + i // 2, x0:x0 + L],
                                  start=True, stop=True)
                m.then_inc(filled, 1)
                ps = claim("ydiag", c)
                pe.wait_ge(mm_ready, c + 1)
                for h in range(HEADS):
                    m = pe.matmul(ps[HD * (h % 2):HD * (h % 2 + 1), L * (h // 2):L * (h // 2 + 1)],
                                  XDT[b][0:L, h, :], MM[b][0:L, h, 0:L], start=True, stop=True)
                m.then_inc(filled, 1)
                ps = claim("state", c)
                pe.wait_ge(xde_ready, c + 1)
                wait_emptied(pe, "bt", c)
                for g in range(2):
                    m = pe.matmul(ps[:, 256 * g:256 * (g + 1)], BT[b][0:L, g, :], XDE[b][0:L, 4 * g:4 * g + 4, :],
                                  start=True, stop=True)
                m.then_inc(filled, 1)
                if c < 4:
                    memory("v_mem", CH_KV, c)
            for s in range(2):
                ps = claim("stout", s)
                wait_emptied(pe, "state", 3 + s)
                for i in range(4):
                    m = turn(ps[:, P * i:P * (i + 1)], ST[s][:, P * i:P * (i + 1)])
                m.then_inc(filled, 1)
            memory("k_mem", CH_KV + 4, 0)
            memory("k_mem", CH_KV + 4, 1)
            ps = claim("ssq")
            for t, (t0, L) in enumerate(TOK):
                pe.wait_ge(squared, t + 1)
                for i in range(4):
                    m = pe.matmul(ps[0:L, t:t + 1], sq[:, i, t0:t0 + L], ones[:, 0:1], start=(i == 0), stop=(i == 3))
            m.then_inc(filled, 1)
            memory("k_mem", CH_KV + 4, 2)
            ps = claim("rbc", 0)
            pe.wait_ge(sn_ready, 1)
            for t, (t0, L) in enumerate(TOK):
                if t == 4:
                    ps = claim("rbc", 1)
                m = pe.matmul(ps[:, L * (t % 4):L * (t % 4 + 1)], sstat[0:L, 3, t:t + 1].to_broadcast([L, P]),
                              ident[0:L, 0:L], start=True, stop=True)
                if t >= 3:
                    m.then_inc(filled, 1)
            def turn_k(stage, k_rows):
                for b in range(4):
                    ps = claim(stage, b)
                    for i in range(2):
                        for t in range(2):
                            kk = 2 * b + i
                            off = MEM * i + P * t
                            m = turn(ps[:, off:off + P], k_rows[:, t, P * kk:P * (kk + 1)])
                    m.then_inc(filled, 1)

            memory("k_mem", CH_KV + 4, 3)
            wait_emptied(pe, "k_mem", 3, 1)
            turn_k("kT", k_tok)

            def token_tile(stage, first_chunk, x, t):
                t0, L = TOK[t]
                for h in range(2):
                    ps = claim(stage, t, h)
                    for cc in range(2):
                        c = first_chunk + 2 * h + cc
                        if t == 0:
                            wait_chunk(pe, c)
                        for k in range(KD):
                            m = pe.matmul(ps[0:L, CW * cc:CW * (cc + 1)], x[:, k, t0:t0 + L], slot(c)[:, k, :],
                                          start=(k == 0), stop=(k == KD - 1))
                    m.then_inc(filled, 1)

            pe.wait_ge(mix_done, 2)
            for t in range(NT):
                token_tile("out", CH_OUT, mix, t)
                if t >= 1:
                    turn_rows("hT", t - 1, NORM_H, TOK[t - 1][1])
            pe.wait_ge(ks_loaded, 16)
            turn_k("ksT", ks_rows)
            wait_chunk(pe, CH_Q)
            wait_emptied(pe, "hT", 2, 1)
            project_half("q", CH_Q, 0, 0, xT)
            turn_rows("hT", NT - 1, NORM_H, TOK[NT - 1][1])
            wait_emptied(pe, "hT", NT - 1, 1)
            for m, h in Q_FIRST:
                if h == 0:
                    wait_chunk(pe, CH_Q + m // 2)
                project_half("q", CH_Q + m // 2, m, h, xT)
            wait_emptied(pe, "q", 3, 1)
            wait_emptied(pe, "ksT", 3)
            pe.wait_ge(attn_loaded, 16)

            def scores(n):
                if n < 2 * NT:
                    t, hp = n % NT, n // NT
                    (t0, L), seq = TOK[t], t // 4
                    ps = claim("score", n)
                    if n in (NT, NT + 2):
                        wait_emptied(pe, "q", 7, (n - NT) // 2)
                    for h in range(2):
                        for k in range(2):
                            kk = 2 * (2 * hp + h) + k
                            m = pe.matmul(ps[0:L, MEM * h:MEM * (h + 1)], mix[:, kk, t0:t0 + L], kT[seq][:, kk, :],
                                          start=(k == 0), stop=(k == 1))
                    m.then_inc(filled, 1)

            def turn_probs(n):
                L, b = TOK[n % NT][1], n % 2
                ps = claim("pT", n)
                pe.wait_ge(pn_ready, n + 1)
                for h in range(2):
                    for k in range(2):
                        i = 2 * h + k
                        m = turn(ps[:, P * i:P * i + L], PR[b][0:L, h, P * k:P * (k + 1)])
                m.then_inc(filled, 1)

            def values(n):
                t, hp, b = n % NT, n // NT, n % 2
                (t0, L), seq = TOK[t], t // 4
                ps = claim("pv", n)
                wait_emptied(pe, "pT", n)
                for h in range(2):
                    for dt_ in range(2):
                        i = 2 * h + dt_
                        d0 = P * (2 * (2 * hp + h) + dt_)
                        for k in range(2):
                            m = pe.matmul(ps[:, P * i:P * i + L], v_tok[seq][:, k, d0:d0 + P],
                                          PT[b][:, 2 * h + k, 0:L], start=(k == 0), stop=(k == 1))
                m.then_inc(filled, 1)

            def o_tile(t):
                wait_emptied(pe, "pv", NT + t)
                token_tile("o", CH_O, mix, t)
                if t >= 1:
                    turn_rows("fT", t - 1, NORM_F, TOK[t - 1][1])

            for n in range(2 * NT + 1):
                if n >= 1:
                    turn_probs(n - 1)
                scores(n)
                if n >= 1:
                    values(n - 1)
                for m, h in Q_FILL.get(n, ()):
                    wait_chunk(pe, CH_Q + m // 2)
                    project_half("q", CH_Q + m // 2, m, h, xT)
                if n >= O_STEP:
                    o_tile(n - O_STEP)
            o_tile(NT - 1)

            pe.wait_ge(route_loaded, 64)

            def route_part(i, last_tile):
                t0, t1 = ROUTE_PARTS[i]
                ps = claim("routef", i)
                wait_emptied(pe, "fT", last_tile, 1)
                for k in range(KD):
                    m = pe.matmul(ps[0:NG + NE, 0:t1 - t0], w_rt[:, k, :], xT[:, k, t0:t1],
                                  start=(k == 0), stop=(k == KD - 1))
                m.then_inc(filled, 1)

            route_part(0, 2)
            turn_rows("fT", NT - 1, NORM_F, TOK[NT - 1][1])
            route_part(1, 3)
            route_part(2, 4)
            ps = claim("route")
            for i, tiles in enumerate(((0, 1), (2, 3), (4,))):
                wait_emptied(pe, "routef", i)
                for t in tiles:
                    t0, L = TOK[t]
                    m = turn(ps[0:L, 36 * t:36 * (t + 1)], lgT[0:NG + NE, t0:t0 + L])
            m.then_inc(filled, 1)
            ps = claim("rank")
            pe.wait_ge(ind_ready, 1)
            pe.matmul(ps[:, 0:NE * (NT + 1)], ones[:, :], before.rearrange("p t e -> p (t e)"), start=True, stop=False)
            pe.matmul(ps[:, 0:NE * (NT + 1)], tri_lt[:, :], ind.rearrange("p t e -> p (t e)"),
                      start=False, stop=True).then_inc(filled, 1)
            for who in ("act", "dve"):
                pe.wait_ge(emptied[who], count[who])

            def turn_x(pp, b):
                pe.wait_ge(gathered[b], 16 * pp + 16)
                for h in range(2):
                    for k in range(4):
                        m = turn(banks[h][:, CAP * k:CAP * (k + 1)], xg[b][0:CAP, 4 * h + k::KD])
                    m.then_inc(turned_x, 1)

            def expert(qq, s, last=False, reused=True):
                b, pp = s % 2, 2 * qq + s // 2
                gate, up = [w.rearrange("p (k n) -> p k n", k=KD) for w in WSET[s][0:2]]
                down = WSET[s][2]
                pe.wait_ge(xT_act, 2 * pp + (b + 1))
                pe.wait_ge(xT_dve, 2 * pp + (b + 1))
                if reused:
                    pe.wait_ge(hid_ready, 2 * pp + b)
                for part, (w, done) in enumerate(((gate, gate_done), (up, gu_done))):
                    wait_expert_chunk(pe, part, qq, s)
                    for j in range(2):
                        for k in range(KD):
                            m = pe.matmul(banks[2 + part][:, CAP * j:CAP * (j + 1)], w[:, k, j::2], xgT[b][:, k, :],
                                          start=(k == 0), stop=(k == KD - 1))
                    m.then_inc(done, 1)
                if not last:
                    turn_x(pp + b, 1 - b)
                pe.wait_ge(hid_ready, 2 * pp + (b + 1))
                wait_expert_chunk(pe, 2, qq, s)
                if reused:
                    pe.wait_ge(yo_act, 2 * pp + (b - 1))
                    pe.wait_ge(yo_dve, 2 * pp + (b - 1))
                for h in range(2):
                    for j in range(2):
                        m = pe.matmul(banks[4 + 2 * b + h][0:CAP, :], hid[b][:, j, :],
                                      down[:, D * j + 512 * h:D * j + 512 * (h + 1)], start=(j == 0), stop=(j == 1))
                    m.then_inc(dn_done, 1)

            def pe_pass(p):
                first = p * QUADS
                again = not isinstance(p, int)
                pe.wait_ge(oh_ready, p + 1)
                for i in range(NT):
                    for k in range(2):
                        m = pe.matmul(banks[0][0:CAP, 0:NE], oh[k][:, i, :], mv[k][:, i, :],
                                      start=(i == 0 and k == 0), stop=(i == NT - 1 and k == 1))
                m.then_inc(slots_filled, 1)
                pe.wait_ge(idx_ready, p + 1)
                turn_x(2 * first, 0)
                for s in range(SETS):
                    expert(first, s, reused=again or s >= 2)
                with pe.Fori(1, QUADS - 1) as i:
                    for s in range(SETS):
                        expert(first + i, s)
                for s in range(SETS):
                    expert(first + (QUADS - 1), s, last=(s == SETS - 1))

            pe_pass(0)
            overflow_passes(pe, pe_pass)

        @block.scalar
        def _(act):
            flat = {"s5_a_re": 0, "s5_a_im": 1, "state_s5_re": 3, "state_s5_im": 4}
            for name, r in flat.items():
                v = a[name] if name[0:5] != "state" else a[name].rearrange("o b g n -> (o b) g n")
                act.dma_start(p_rows[0:16, r, :].rearrange("q (g n) -> q g n", g=2),
                              v.rearrange("o (q g) n -> (o q) g n", g=2)).then_inc(par_loaded, 16)
            act.dma_start(ld_rows[0:16, :], a["s5_log_dt"].rearrange("o (q g) -> (o q) g", g=2)).then_inc(par_loaded, 16)
            act.dma_start(s5d_rows[0:16, :], a["s5_d"].rearrange("o (q g) c -> (o q) (g c)", g=2)).then_inc(par_loaded, 16)

            def copy_out(dst, src, *key, scale=1.0, func=ACT.Copy):
                act.activation(dst, src, func, scale=scale).then_inc(emptied["act"], 1)

            def rstd(n):
                L = norm_len(n)
                act.wait_ge(ms_ready, n + 1)
                act.activation(stat[0:L, n, 16:17], stat[0:L, n, 15:16], ACT.Sqrt).then_inc(rstd_ready, 1)

            def turned(stage, t, dst, t0, L):
                for h in range(2):
                    ps = wait_filled(act, stage, t, h)
                    copy_out(dst[:, 4 * h:4 * h + 4, t0:t0 + L], ps[:, :].rearrange("p (k l) -> p k l", k=4)[:, :, 0:L])

            asks = [0]

            def small(out, in_, func, scale=1.0, last=True):
                if last:
                    asks[0] += 1
                act.activation(out, in_, func, scale=scale).then_inc(small_done, 1)

            rstd(0)
            for ri, name in enumerate(("s5_b_re", "s5_b_im")):
                act.dma_start(b_raw[:, ri], a[name].rearrange("o (q g) n c -> (o g n) q c", g=2)).then_inc(s5_loaded, 16)
            for ri, name in enumerate(("s5_c_re", "s5_c_im")):
                for copy in range(2):
                    act.dma_start(c_rows[:, ri, :, copy, :], a[name].rearrange("o g c n -> (o g c) n")
                                  .rearrange("(i r) n -> r i n", r=P)).then_inc(s5_loaded, 16)
            rstd(1)
            turned("xT", 0, xT, *TOK[0])
            rstd(2)
            turned("xT", 1, xT, *TOK[1])
            def copy_u(mt, h):
                ps = wait_filled(act, "u", mt, h)
                copy_out(uT[:, mt, HALF * h:HALF * (h + 1)], ps[:, 0:HALF])

            turned("xT", 2, xT, *TOK[2])
            rstd(3)
            copy_u(0, 0)
            rstd(4)
            for ri in range(2):
                ps = wait_filled(act, "cT", ri)
                for g2 in range(2):
                    half = slice(SN * g2, SN * (g2 + 1))
                    src = ps[half, :].rearrange("p (q g c) -> p q g c", g=2, c=GC)[:, :, g2, :]
                    if ri == 0:
                        act.activation(c_t[half, 0], src, ACT.Copy)
                        m = act.activation(c_t[half, 1], src, ACT.Copy, scale=-1.0)
                    else:
                        m = act.activation(c_t[half, 2], src, ACT.Copy, scale=-1.0)
                m.then_inc(emptied["act"], 1)
            copy_u(1, 0)
            turned("xT", 3, xT, *TOK[3])
            turned("xT", 4, xT, *TOK[4])
            act.wait_ge(small_ask, 1)
            small(s5s[:, 0, :], s5p[:, 2, :], ACT.Exp)
            act.wait_ge(small_ask, 2)
            small(s5s[:, 3, :], s5s[:, 1, :], ACT.Exp)
            act.wait_ge(small_ask, 3)
            act.activation(s5s[:, 8, :], s5s[:, 7, :], ACT.Sin)
            small(s5s[:, 9, :], s5s[:, 7, :], ACT.Sin, scale=0.5)
            for mt in range(2, 4):
                copy_u(mt, 0)
            for mt in range(4):
                copy_u(mt, 1)
            for b in range(0, 8, 2):
                ps = wait_filled(act, "wT", b)
                copy_out(WT[:, 2 * b:2 * b + 2].rearrange("p q r n -> p (q r n)"), ps[:, :])
            def copy_z(mt, h):
                ps = wait_filled(act, "z", mt, h)
                copy_out(mix[:, mt, HALF * h:HALF * (h + 1)], ps[:, 0:HALF], func=ACT.Silu)

            for i in range(4):
                for h in range(2):
                    ps = wait_filled(act, "uj", i, h)
                    copy_out(Uj[0:NJ, i % 2].rearrange("p g (k c) -> p k g c", c=GC)[:, 4 * h:4 * h + 4],
                             ps[0:NJ, :].rearrange("p (k g c) -> p k g c", k=4, c=GC))
                if i == 0:
                    act.wait_ge(G_ready, 1)
                copy_z(i // 2, i % 2)
            for b in range(4):
                ps = wait_filled(act, "tap", b)
                copy_out(tap[0:32, 4 * b:4 * b + 4, :].rearrange("p k c -> p (k c)"), ps[0:32, :])
            for h in range(2):
                ps = wait_filled(act, "dtf", h)
                copy_out(dtT[:, HALF * h:HALF * (h + 1)], ps[0:HEADS, 0:HALF])
            act.wait_ge(small_loaded, 16 * SMALL_LOADS)
            act.wait_ge(small_ask, 4)
            act.activation(dtt[:, 2, 0:HEADS], a_lg[:, :], ACT.Exp)
            small(dtt[:, 1, :], dtt[:, 0, :], ACT.Exp, scale=-1.0)
            act.wait_ge(small_ask, 5)
            small(dtt[:, 4, :], dtt[:, 3, :], ACT.Ln)
            act.wait_ge(G_ready, 1)
            act.wait_ge(R_ready, 1)

            def conv_silu(i):
                act.wait_ge(conv_sum, i + 1)
                act.activation(xbc[:, i, 0:NP], cv[i % 2][:, 0:NP], ACT.Silu)
                act.activation(xbc[:, i, SAMPLE_COL:CONV_OUT], cv[i % 2][:, SAMPLE_COL:CONV_OUT], ACT.Silu)\
                    .then_inc(conv_done, 1)

            for i in range(8):
                ps = wait_filled(act, "xbc", i, 0)
                copy_out(xbc[:, i, 3:3 + HALF], ps[:, 0:HALF])
                ps = wait_filled(act, "xbc", i, 1)
                act.activation(xbc[:, i, 3 + HALF:3 + NP], ps[:, 0:NP - HALF], ACT.Copy)
                copy_out(xbc[:, i, NP + 6:CONV_COLS], ps[:, NP - HALF:HALF])
                if i >= 2:
                    conv_silu(i - 2)
                if i == 0:
                    act.wait_ge(conv_pad, 1)
                wait_emptied(act, "xbc", i, 1)
                if i >= 2:
                    act.wait_ge(conv_done, i - 1)
                act.activation(cv[i % 2], xbc[:, i, 0:CONV_OUT], ACT.Identity, scale=vecT[:, i, 0:1],
                               bias=vecT[:, i, 4:5]).then_inc(conv_first, 1)
            conv_silu(6)
            conv_silu(7)
            rstd(5)
            rstd(6)
            for mt in range(2, 4):
                for h in range(2):
                    copy_z(mt, h)
            for i in range(4):
                for g2 in range(2):
                    ps = wait_filled(act, "y", i, g2)
                    copy_out(Yj[0:NJ, i % 2].rearrange("p s (q g c) -> p q g s c", g=2, c=GC)[:, :, g2],
                             ps[0:NJ, :].rearrange("p (q s c) -> p q s c", q=4, c=GC), func=ACT.Gelu_apprx_tanh)
            for mt in range(4):
                for h in range(2):
                    ps = wait_filled(act, "glu", mt, h)
                    copy_out(sig[:, mt, HALF * h:HALF * (h + 1)], ps[:, 0:HALF], func=ACT.Sigmoid)
            ps = wait_filled(act, "s5fin")
            copy_out(s5row[0:16].rearrange("p k n -> p (k n)"), ps[0:16, :])
            wait_emptied(act, "s5fin")
            for k, name in enumerate(("s5_re_p", "s5_im_p", "s5_re_s", "s5_im_s")):
                act.dma_start(o[name].rearrange("a b (q g) n -> (a b q) (g n)", g=2), s5row[0:16, k, :])\
                   .then_inc(mix_stored, 16)
            for b in range(2):
                for h in range(2):
                    ps = wait_filled(act, "convT", b, h)
                    copy_out(conv_rows[0:3, b, 512 * h:512 * (h + 1)], ps[0:3, :])
            wait_emptied(act, "convT", 1, 1)
            for b, name in enumerate(("conv_p", "conv_s")):
                act.dma_start(o[name].rearrange("a b k c -> (a b k) c"), conv_rows[0:3, b, :]).then_inc(mix_stored, 16)

            def prep(c):
                (t0, L), b = TOK[c], c % 2
                ps = wait_filled(act, "tot", c)
                if c >= 2:
                    act.wait_ge(xde_ready, c - 1)
                    wait_emptied(act, "state", c - 2)
                act.activation(expo[0:L, b, 0:HEADS], ps[0:L, 0:HEADS], ACT.Exp)
                copy_out(expo[:, b, HEADS:2 * HEADS], ps[:, HEADS:2 * HEADS], func=ACT.Exp)
                ps = wait_filled(act, "cs", c)
                if c >= 2:
                    act.wait_ge(y_gated, c - 1)
                copy_out(EC[b][:, :, 0:L], ps[:, 0:4 * L].rearrange("p (i l) -> p i l", i=4), func=ACT.Exp)
                for hg in range(2):
                    ps = wait_filled(act, "seg", c, hg)
                    if c >= 2:
                        act.wait_ge(filled, job[("ydiag", c - 2)] + 1)
                    copy_out(MM[b][0:L, 4 * hg:4 * hg + 4, 0:L], ps[0:L, 0:4 * L].rearrange("p (i l) -> p i l", i=4),
                             func=ACT.Exp)
                ps = wait_filled(act, "bt", c)
                if c >= 2:
                    act.wait_ge(filled, job[("state", c - 2)] + 1)
                copy_out(BT[b][0:L], ps[0:L, 0:256].rearrange("p (g n) -> p g n", g=2))

            def copy_memory(stage, dst, c):
                for t in range(2):
                    ps = wait_filled(act, stage, c, t)
                    copy_out(dst[:, t, CW * c:CW * (c + 1)], ps[:, 0:CW])

            def store_memory(stage, src, name):
                wait_emptied(act, stage, 3, 1)
                act.dma_start(o[name].rearrange("a b m h d -> (a b m) (h d)").rearrange("(t q) n -> q t n", q=P), src)\
                   .then_inc(kv_stored, 16)

            prep(0)
            for t in range(2):
                turned("memT", t, mnT, P * t, P)
            for c, (t0, L) in enumerate(TOK):
                if c + 1 < NT:
                    prep(c + 1)
                act.wait_ge(y_gated, c + 1)
                if c == 0:
                    act.wait_ge(mix_done, 1)
                act.activation(sq[:, :, t0:t0 + L], mix[:, 0:4, t0:t0 + L], ACT.Square).then_inc(squared, 1)
                if c < 4:
                    copy_memory("v_mem", v_tok[0], c)
            store_memory("v_mem", v_tok[0], "mem_v_p")
            for s, name in enumerate(("ssd_p", "ssd_s")):
                ps = wait_filled(act, "stout", s)
                copy_out(st_out[s].rearrange("p i n -> p (i n)"), ps[:, :])
                wait_emptied(act, "stout", s)
                act.dma_start(o[name].rearrange("a b h p n -> (a b h p) n").rearrange("(i q) n -> q i n", q=P),
                              st_out[s]).then_inc(st_stored, 16)
            copy_memory("k_mem", k_tok, 0)
            copy_memory("k_mem", k_tok, 1)
            act.wait_ge(small_ask, 6)
            act.activation(sstat[:, 3, :], sstat[:, 2, :], ACT.Sqrt).then_inc(sn_ready, 1)
            for c in range(2, 4):
                copy_memory("k_mem", k_tok, c)
            store_memory("k_mem", k_tok, "mem_k_p")
            act.wait_ge(mix_stored, 16 * 6)
            for b in range(4):
                ps = wait_filled(act, "kT", b)
                copy_out(kT[0][:, 2 * b:2 * b + 2, :].rearrange("p k m -> p (k m)"), ps[:, :])
            act.wait_ge(kv_stored, 32)
            for t in range(NT - 1):
                rstd(NORM_H + t)
                turned("hT", t, xT, *TOK[t])
            rstd(NORM_H + NT - 1)
            for b in range(4):
                ps = wait_filled(act, "ksT", b)
                copy_out(kT[1][:, 2 * b:2 * b + 2, :].rearrange("p k m -> p (k m)"), ps[:, :])

            def copy_q(mt, h):
                ps = wait_filled(act, "q", mt, h)
                copy_out(mix[:, mt, HALF * h:HALF * (h + 1)], ps[:, 0:HALF], scale=XD ** -0.5)

            copy_q(0, 0)
            turned("hT", NT - 1, xT, *TOK[NT - 1])
            for mt, h in Q_FIRST:
                copy_q(mt, h)

            def probs(n):
                L, b = TOK[n % NT][1], n % 2
                act.wait_ge(mx_ready, n + 1)
                if n >= 2:
                    act.wait_ge(filled, job[("pT", n - 2)] + 1)
                ps = bank_of("score", n)
                for h in range(2):
                    m = act.activation(PR[b][0:L, h, :], ps[0:L, MEM * h:MEM * (h + 1)], ACT.Exp,
                                       bias=amax[0:L, n, h:h + 1], accum_out=asum[0:L, n, h:h + 1])
                m.then_inc(emptied["act"], 1)

            def o_tile(t):
                t0, L = TOK[t]
                rstd(NORM_F + t)
                act.wait_ge(normed, NORM_F + t + 1)
                act.dma_start(xf_dram[t0:t0 + L, :], rows[0:L, t % 3, :]).then_inc(f_stored[t % 3], 16)

            for n in range(2 * NT + 1):
                if n >= 1:
                    L, b = TOK[(n - 1) % NT][1], (n - 1) % 2
                    ps = wait_filled(act, "pT", n - 1)
                    if n >= 3:
                        act.wait_ge(filled, job[("pv", n - 3)] + 1)
                    copy_out(PT[b][:, :, 0:L], ps[:, :].rearrange("p (i l) -> p i l", i=4)[:, :, 0:L])
                if n > O_STEP:
                    o_tile(n - O_STEP - 1)
                if n < 2 * NT:
                    probs(n)
                for m, h in Q_FILL.get(n, ()):
                    copy_q(m, h)
                if n > O_STEP:
                    turned("fT", n - O_STEP - 1, xT, *TOK[n - O_STEP - 1])
            o_tile(NT - 2)
            turned("fT", NT - 2, xT, *TOK[NT - 2])
            o_tile(NT - 1)

            def copy_route(i):
                t0, t1 = ROUTE_PARTS[i]
                ps = wait_filled(act, "routef", i)
                copy_out(lgT[0:NG + NE, t0:t1], ps[0:NG + NE, 0:t1 - t0])

            copy_route(0)
            turned("fT", NT - 1, xT, *TOK[NT - 1])
            copy_route(1)
            copy_route(2)
            act.wait_ge(route_ask, 1)
            act.activation(r_gl, r_gl, ACT.Exp)
            act.activation(r_d, r_d, ACT.Exp).then_inc(route_done, 1)

            def copy_x(pp, b):
                act.wait_ge(turned_x, 4 * pp + (2 * b + 1))
                act.activation(xgT[b][:, 0:4, :].rearrange("p k l -> p (k l)"), banks[0][:, 0:4 * CAP], ACT.Copy)\
                    .then_inc(xT_act, 1)

            def act_expert(pp, b, last=False, reused=True):
                act.wait_ge(gate_done, 2 * pp + (b + 1))
                act.activation(gact[b].rearrange("p j l -> p (j l)"), banks[2][:, 0:2 * CAP], ACT.Silu)\
                    .then_inc(silu_done, 1)
                if not last:
                    copy_x(pp + b, 1 - b)
                act.wait_ge(dn_done, 4 * pp + (2 * b + 1))
                if reused:
                    act.wait_ge(scattered[b], 16 * pp)
                act.activation(yo[b][0:CAP, 0:512], banks[4 + 2 * b][0:CAP, :], ACT.Copy).then_inc(yo_act, 1)

            def act_pass(p):
                first = p * (LAST + 1)
                again = not isinstance(p, int)
                copy_x(first, 0)
                for b in range(2):
                    act_expert(first, b, reused=again)
                with act.Fori(1, LAST) as i:
                    for b in range(2):
                        act_expert(first + i, b)
                for b in range(2):
                    act_expert(first + LAST, b, last=(b == 1))

            act_pass(0)
            overflow_passes(act, act_pass)
            for t in range(NT + 1):
                if t < NT:
                    L, k = TOK[t][1], NORM_Y + t
                    act.wait_ge(h_final, t + 1)
                    act.activation(y2[t][0:L, 0, :], H[0:L, t, :], ACT.Square, accum_out=stat[0:L, k, 14:15])\
                        .then_inc(h_squared, 1)
                if t >= 1:
                    L, k = TOK[t - 1][1], NORM_Y + t - 1
                    rstd(k)
                    if t - 1 < Y_POOL:
                        act.wait_ge(rstd_ready, k + 1)
                        act.activation(rows[0:L, t - 1, :], H[0:L, t - 1, :], ACT.Copy, scale=stat[0:L, k, 16:17])\
                            .then_inc(y_scaled, 1)

        @block.vector
        def _(dve):
            n = [0]

            def step(ins):
                n[0] += 1
                return ins.then_inc(dstep, 1)

            def sync():
                dve.wait_ge(dstep, n[0])

            def link(ins):
                step(ins)
                sync()

            def tt(out, x, y, op=ALU.mult):
                return dve.tensor_tensor(out, x, y, op)

            def copy_out(dst, src):
                dve.tensor_copy(dst, src).then_inc(emptied["dve"], 1)

            def stats(k, x, L):
                for h in range(2):
                    step(dve.bn_stats(stat[0:L, k, 6 * h:6 * h + 6], x[:, 512 * h:512 * (h + 1)]))
                sync()
                link(dve.bn_aggr(stat[0:L, k, 12:14], stat[0:L, k, 0:12]))
                link(dve.scalar_tensor_tensor(stat[0:L, k, 14:15], stat[0:L, k, 12:13], stat[0:L, k, 12:13],
                                              stat[0:L, k, 13:14], ALU.mult, ALU.add))
                link(dve.tensor_scalar(stat[0:L, k, 17:18], stat[0:L, k, 14:15], EPS, None, ALU.add))
                dve.reciprocal(stat[0:L, k, 15:16], stat[0:L, k, 17:18]).then_inc(ms_ready, 1)

            def scale_rows(k, out, x, g, L):
                dve.wait_ge(rstd_ready, k + 1)
                dve.scalar_tensor_tensor(out, x, stat[0:L, k, 16:17], gain[0:L, g, :], ALU.mult, ALU.mult)\
                    .then_inc(normed, 1)

            def row_stats(k):
                dve.wait_ge(row_loaded[ROW_SLOT[k]], 16 * ROW_TURN[k])
                stats(k, rows[0:staged[k][1], ROW_SLOT[k], :], staged[k][1])

            def row_scale(k, g):
                x = rows[0:staged[k][1], ROW_SLOT[k], :]
                scale_rows(k, x, x, g, staged[k][1])

            dve.wait_ge(gain_loaded[0], 16)
            for k in range(3):
                row_stats(k)
                row_scale(k, 0)
            ps = wait_filled(dve, "vec")
            copy_out(vecT[:, :, :].rearrange("p k v -> p (k v)"), ps[:, 0:72])
            ps = wait_filled(dve, "s5par")
            step(dve.tensor_copy(s5d[:, :], ps[0:2 * GC, 80:96]))
            copy_out(s5p[:, :, :].rearrange("p k v -> p (k v)"), ps[:, 0:80])
            wait_emptied(dve, "s5par")
            dve.tensor_copy(s5s[:, 18, :], s5p[:, 2, :]).then_inc(small_ask, 1)
            for k in range(3, NT):
                row_stats(k)
            for k in range(3, NT):
                row_scale(k, 0)

            s = s5s
            are, aim = s5p[:, 0, :], s5p[:, 1, :]
            dve.wait_ge(small_done, 1)
            step(tt(s[:, 2, :], aim, s[:, 0, :]))
            tt(s[:, 1, :], are, s[:, 0, :]).then_inc(small_ask, 1)
            sync()
            link(dve.tensor_scalar(s[:, 4, :], s[:, 2, :], 1.0 / TWO_PI, MAGIC, ALU.mult, ALU.add))
            link(dve.tensor_scalar(s[:, 5, :], s[:, 4, :], MAGIC, None, ALU.subtract))
            link(dve.scalar_tensor_tensor(s[:, 4, :], s[:, 5, :], -PI_A, s[:, 2, :], ALU.mult, ALU.add))
            link(dve.scalar_tensor_tensor(s[:, 6, :], s[:, 5, :], -PI_B, s[:, 4, :], ALU.mult, ALU.add))
            link(dve.scalar_tensor_tensor(s[:, 4, :], s[:, 5, :], -PI_C, s[:, 6, :], ALU.mult, ALU.add))
            dve.tensor_scalar(s[:, 7, :], s[:, 4, :], 3.1415925, -3.1415925, ALU.min, ALU.max).then_inc(small_ask, 1)
            step(dve.memset(powr[:, 0, :], 1.0))
            step(dve.memset(powi[:, 0, :], 0.0))
            step(tt(s[:, 10, :], are, are))
            step(tt(s[:, 11, :], aim, aim))
            sync()
            link(tt(s[:, 10, :], s[:, 10, :], s[:, 11, :], ALU.add))
            link(dve.reciprocal(s[:, 12, :], s[:, 10, :]))
            dve.wait_ge(small_done, 3)
            link(tt(s[:, 13, :], s[:, 9, :], s[:, 9, :]))
            link(dve.tensor_scalar(s[:, 13, :], s[:, 13, :], -2.0, 1.0, ALU.mult, ALU.add))
            step(tt(powr[:, 1, :], s[:, 3, :], s[:, 13, :]))
            step(tt(powi[:, 1, :], s[:, 3, :], s[:, 8, :]))
            sync()

            def cmul(outr, outi, ar, ai, br, bi, t):
                step(tt(t[0], ar, br))
                step(tt(t[1], ai, bi))
                step(tt(t[2], ar, bi))
                step(tt(t[3], ai, br))
                sync()
                step(tt(outr, t[0], t[1], ALU.subtract))
                step(tt(outi, t[2], t[3], ALU.add))
                sync()

            def rep(v, m):
                return v.unsqueeze(1).to_broadcast([P, m, PAIRS])

            for m in (1, 2, 4):
                t4 = [prod_b[:, 64 * i:64 * i + PAIRS * m].rearrange("p (k q) -> p k q", k=m) for i in range(4)]
                cmul(powr[:, m + 1:2 * m + 1, :], powi[:, m + 1:2 * m + 1, :], powr[:, 1:m + 1, :], powi[:, 1:m + 1, :],
                     rep(powr[:, m, :], m), rep(powi[:, m, :], m), t4)
            step(dve.tensor_copy(supr[:, 0, :], powr[:, 8, :]))
            dve.tensor_copy(supi[:, 0, :], powi[:, 8, :]).then_inc(lam_ready, 1)
            link(dve.tensor_scalar(s[:, 14, :], powr[:, 1, :], -1.0, None, ALU.add))
            step(tt(s[:, 15, :], s[:, 14, :], are))
            step(tt(s[:, 16, :], powi[:, 1, :], aim))
            step(tt(s[:, 17, :], powi[:, 1, :], are))
            step(tt(s[:, 11, :], s[:, 14, :], aim))
            sync()
            step(tt(s[:, 15, :], s[:, 15, :], s[:, 16, :], ALU.add))
            step(tt(s[:, 17, :], s[:, 17, :], s[:, 11, :], ALU.subtract))
            sync()
            step(tt(s[:, 15, :], s[:, 15, :], s[:, 12, :]))
            step(tt(s[:, 17, :], s[:, 17, :], s[:, 12, :]))
            sync()

            dve.wait_ge(s5_loaded, 16 * S5_LOADS)
            fr = s[:, 15, :].unsqueeze(2).to_broadcast([P, PAIRS, GC])
            fi = s[:, 17, :].unsqueeze(2).to_broadcast([P, PAIRS, GC])
            t4 = [prod_b[:, 256 * i:256 * (i + 1)].rearrange("p (q c) -> p q c", q=PAIRS) for i in range(4)]
            cmul(bb[:, 0], bb[:, 1], b_raw[:, 0], b_raw[:, 1], fr, fi, t4)
            tmp = prod_b[:, 0:2048].rearrange("p (q k c) -> p q k c", q=PAIRS, k=8)

            def lam_k(v):
                return v[:, 0:8, :].rearrange("p k q -> p q k").unsqueeze(3).to_broadcast([P, PAIRS, 8, GC])

            def b_k(v):
                return v.unsqueeze(2).to_broadcast([P, PAIRS, 8, GC])

            for ri in range(2):
                step(tt(R[:, ri], lam_k(powr), b_k(bb[:, ri])))
                step(tt(tmp, lam_k(powi), b_k(bb[:, 1 - ri])))
                sync()
                if ri == 0:
                    link(tt(R[:, 0], R[:, 0], tmp, ALU.subtract))
                else:
                    tt(R[:, 1], R[:, 1], tmp, ALU.add).then_inc(R_ready, 1)
            dve.wait_ge(consts, 1)
            for ri in range(2):
                for g2 in range(2):
                    half = slice(SN * g2, SN * (g2 + 1))
                    dve.tensor_copy(bd[half, ri, :, GC * g2:GC * (g2 + 1)], bb[half, ri]).then_inc(bd_ready, 1)
            for m in (1, 2, 4):
                t4 = [s[:, i * 4:i * 4 + m, :] for i in range(4)]
                cmul(supr[:, m:2 * m, :], supi[:, m:2 * m, :], supr[:, 0:m, :], supi[:, 0:m, :],
                     rep(supr[:, m - 1, :], m), rep(supi[:, m - 1, :], m), t4)
            for r in range(2):
                step(dve.tensor_copy(l8a[:, PAIRS * r:PAIRS * (r + 1)], supr[:, 0, :]))
            step(dve.tensor_scalar(l8b[:, 0:PAIRS], supi[:, 0, :], -1.0, None, ALU.mult))
            step(dve.tensor_copy(l8b[:, PAIRS:], supi[:, 0, :]))
            h0 = s5p[:, 3:5, :]
            step(tt(s[:, 16, :], supr[:, 0, :], h0[:, 0, :]))
            step(tt(s[:, 17, :], supi[:, 0, :], h0[:, 1, :]))
            step(tt(s[:, 14, :], supr[:, 0, :], h0[:, 1, :]))
            step(tt(s[:, 15, :], supi[:, 0, :], h0[:, 0, :]))
            sync()
            link(tt(s[:, 16, :], s[:, 16, :], s[:, 17, :], ALU.subtract))
            link(tt(s[:, 17, :], s[:, 14, :], s[:, 15, :], ALU.add))
            link(tt(i16[:, :], ident[0:32, 0:GC], ident[0:32, GC:2 * GC], ALU.add))
            link(tt(dti[:, :].rearrange("p (q c) -> p q c", q=PAIRS), s5d[:, :].unsqueeze(2).to_broadcast([32, PAIRS, GC]),
                    i16[:, :].unsqueeze(1).to_broadcast([32, PAIRS, GC])))
            for b in range(1, 8, 2):
                ps = wait_filled(dve, "wT", b)
                copy_out(WT[:, 2 * b:2 * b + 2].rearrange("p q r n -> p (q r n)"), ps[:, :])
            for i in range(4):
                for h in range(2):
                    ps = wait_filled(dve, "ug", i, h)
                    copy_out(U[:, 8 * i + 4 * h:8 * i + 4 * h + 4, :].rearrange("p g j -> p (g j)"), ps[:, 0:4 * NJ])
            SSr = SS.rearrange("p (r q) j -> p q r j", r=2)
            for b in range(8):
                ps = wait_filled(dve, "v", b)
                copy_out(SSr[:, 2 * b:2 * b + 2, :, 1:NJ + 1],
                         ps[:, 0:4 * NJ].rearrange("p (q r j) -> p q r j", q=2, r=2))
            wait_emptied(dve, "v", 7)
            step(dve.memset(SS[:, :, 0:1], 0.0))
            first = SS[:, :, 65:66].rearrange("p a o -> p (a o)")
            link(tt(first, first, s[:, 16:18, :].rearrange("p r q -> p (r q)"), ALU.add))

            def lam8_step(dst, src, m):
                def wide(v, lo, hi):
                    return v[:, lo:hi].unsqueeze(2).to_broadcast([P, hi - lo, m])
                step(tt(h1[:, :, 0:m], src, wide(l8a, 0, 2 * PAIRS)))
                step(tt(h2[:, 0:PAIRS, 0:m], src[:, PAIRS:, :], wide(l8b, 0, PAIRS)))
                step(tt(h2[:, PAIRS:, 0:m], src[:, 0:PAIRS, :], wide(l8b, PAIRS, 2 * PAIRS)))
                sync()
                link(tt(h3[:, :, 0:m], h1[:, :, 0:m], h2[:, :, 0:m], ALU.add))
                link(tt(dst, dst, h3[:, :, 0:m], ALU.add))

            wait_emptied(dve, "tap", 3)
            tap0 = tap[0:32, :, 0:GC]
            tt(tap0, tap0, dti[:, :].rearrange("p (q c) -> p q c", q=PAIRS), ALU.add).then_inc(tap_ready, 1)
            d = dtt
            ps = wait_filled(dve, "dt")
            dve.wait_ge(small_loaded, 16 * SMALL_LOADS)
            for par in range(2):
                half = slice(HD * par, HD * (par + 1))
                step(dve.tensor_copy(dsk[half, :], dsk_rows[half, par::2]))
            link(dve.memset(d[:, 5, :], 0.0))
            raw = d[:, 5, :].rearrange("p (t h) -> p t h", t=NT)
            step(tt(raw[:, 0:4, :], ps[:, 0:32].rearrange("p (t h) -> p t h", t=4),
                    dt_b[:, :].unsqueeze(1).to_broadcast([P, 4, HEADS]), ALU.add))
            tt(raw[0:NS, 4, :], ps[0:NS, 32:40], dt_b[0:NS, :], ALU.add).then_inc(emptied["dve"], 1)
            sync()
            wait_emptied(dve, "dt")
            dve.scalar_tensor_tensor(d[:, 0, :], d[:, 5, :], -1.0, d[:, 5, :], ALU.mult, ALU.max).then_inc(small_ask, 1)
            dve.wait_ge(small_done, 4)
            link(dve.tensor_scalar(d[:, 3, :], d[:, 1, :], 1.0, None, ALU.add))
            dve.tensor_scalar(d[:, 6, :], d[:, 3, :], 1.0, None, ALU.subtract).then_inc(small_ask, 1)
            step(dve.tensor_scalar(d[:, 0, :], d[:, 3, :], 1.0, None, ALU.is_equal))
            sync()
            dve.wait_ge(small_ask, 5)
            link(tt(d[:, 6, :], d[:, 6, :], d[:, 0, :], ALU.add))
            link(dve.reciprocal(dt_v[:, :, :].rearrange("p t h -> p (t h)"), d[:, 6, :]))
            dvf = dt_v[:, :, :].rearrange("p t h -> p (t h)")
            link(tt(dvf, dvf, d[:, 1, :]))
            dve.wait_ge(small_done, 5)
            link(tt(dvf, dvf, d[:, 4, :]))
            link(tt(d[:, 0, :], d[:, 0, :], d[:, 1, :]))
            link(tt(dvf, dvf, d[:, 0, :], ALU.add))
            link(dve.scalar_tensor_tensor(dvf, d[:, 5, :], 0.0, dvf, ALU.max, ALU.add))
            dve.scalar_tensor_tensor(da_v[:, :, :], dt_v[:, :, :], -1.0,
                                     d[:, 2, 0:HEADS].unsqueeze(1).to_broadcast([P, NT, HEADS]), ALU.mult, ALU.mult)\
                .then_inc(da_ready, 1)
            for i in range(1, 8):
                lam8_step(SSc[:, :, :, i], SSc[:, :, :, i - 1], SUP)
            step(dve.tensor_copy(l8a[:, 0:PAIRS], supr[:, 7, :]))
            step(dve.tensor_copy(l8a[:, PAIRS:], supr[:, 7, :]))
            step(dve.tensor_scalar(l8b[:, 0:PAIRS], supi[:, 7, :], -1.0, None, ALU.mult))
            step(dve.tensor_copy(l8b[:, PAIRS:], supi[:, 7, :]))
            sync()
            for c in range(1, SUP - 1):
                lam8_step(SSc[:, :, c, 7:8], SSc[:, :, c - 1, 7:8], 1)
            f1 = rows[:, 0, 0:16 * 49].rearrange("p (q s i) -> p q s i", q=PAIRS, s=7)
            f2 = rows[:, 1, 0:16 * 49].rearrange("p (q s i) -> p q s i", q=PAIRS, s=7)
            wait_filled(dve, "xT", 4, 1)

            def pw(v):
                return v[:, 0:7, :].rearrange("p i q -> p q i").unsqueeze(2).to_broadcast([P, PAIRS, 7, 7])

            def carry(r):
                return SSc[:, PAIRS * r:PAIRS * (r + 1), 0:7, 7:8].to_broadcast([P, PAIRS, 7, 7])

            for r in range(2):
                dst = SSc[:, PAIRS * r:PAIRS * (r + 1), 1:8, 0:7]
                step(tt(f1, pw(supr), carry(r)))
                step(tt(f2, pw(supi), carry(1 - r)))
                sync()
                link(tt(dst, dst, f1, ALU.add))
                link(tt(dst, dst, f2, ALU.subtract if r == 0 else ALU.add))
            fin = s5f[:, :, :].rearrange("p (b r) q -> p b (r q)", b=2)
            step(dve.tensor_copy(fin[:, 0, :], SS[:, :, 64]))
            step(dve.tensor_copy(fin[:, 1, :], SS[:, :, 72]))
            sync()
            dve.tensor_copy(SS[:, :, 64], s5p[:, 3:5, :].rearrange("p r q -> p (r q)")).then_inc(h_ready, 1)

            for i in range(8):
                dve.wait_ge(conv_first, i + 1)
                for k in range(1, CONV_K):
                    ins = dve.scalar_tensor_tensor(cv[i % 2], xbc[:, i, k:k + CONV_OUT], vecT[:, i, k:k + 1], cv[i % 2],
                                                   ALU.mult, ALU.add)
                    if k < CONV_K - 1:
                        link(ins)
                    else:
                        ins.then_inc(conv_sum, 1)
            dve.wait_ge(gain_loaded[1], 16)
            row_stats(5)
            row_stats(6)
            row_scale(5, 1)
            row_scale(6, 1)

            for i in range(4):
                for h in range(2):
                    ps = wait_filled(dve, "yT", i, h)
                    copy_out(mix[:, 4 + i, :].rearrange("p (j l) -> p l j", l=Q8)[:, 4 * h:4 * h + 4, :],
                             ps[:, 0:4 * NJ].rearrange("p (l j) -> p l j", l=4))
            wait_emptied(dve, "glu", 3, 1)
            for i in range(4):
                ins = tt(mix[:, 4 + i, :], mix[:, 4 + i, :], sig[:, i, :])
            ins.then_inc(mix_done, 1)

            ps = wait_filled(dve, "stin")
            copy_out(ST[1], ps[:, :])
            dve.memset(ST[0], 0.0).then_inc(st_ready, 1)

            def prep(c):
                (t0, L), b = TOK[c], c % 2
                ps = wait_filled(dve, "cb", c)
                dve.tensor_tensor(CB[b][0:L, :, 0:L], ps[0:L, 0:2 * L].rearrange("p (g l) -> p g l", g=2),
                                  tri_le[0:L, 0:L].unsqueeze(1).to_broadcast([L, 2, L]), ALU.mult)\
                    .then_inc(emptied["dve"], 1)
                ps = wait_filled(dve, "xs", c)
                if c >= 2:
                    dve.wait_ge(xde_ready, c - 1)
                    dve.wait_ge(filled, job[("ydiag", c - 2)] + 1)
                dve.tensor_tensor(XDT[b][0:L], ps[0:L, :].rearrange("p (h d) -> p h d", h=HEADS),
                                  dt_v[0:L, c, :].unsqueeze(2).to_broadcast([L, HEADS, HD]), ALU.mult)\
                    .then_inc(emptied["dve"], 1)
                wait_emptied(dve, "xs", c)
                wait_emptied(dve, "seg", c, 1)
                m4 = MM[b][0:L, :, 0:L].rearrange("p (g h) l -> p g h l", g=2)
                dve.tensor_tensor(m4, m4, CB[b][0:L, :, 0:L].unsqueeze(2).to_broadcast([L, 2, 4, L]), ALU.mult)\
                    .then_inc(mm_ready, 1)

            prep(0)
            for c, (t0, L) in enumerate(TOK):
                if c + 1 < NT:
                    prep(c + 1)
                b, st = c % 2, ST[c // 4]
                ac = acc[:, :, 0:L]
                ps = wait_filled(dve, "yoff", c)
                wait_emptied(dve, "cs", c)
                tt(ac, ps[:, 0:4 * L].rearrange("p (i l) -> p i l", i=4), EC[b][:, :, 0:L]).then_inc(emptied["dve"], 1)
                ps = wait_filled(dve, "ydiag", c)
                wait_emptied(dve, "yoff", c)
                tt(ac, ps[:, 0:4 * L].rearrange("p (i l) -> p i l", i=4), ac, ALU.add).then_inc(emptied["dve"], 1)
                dve.wait_ge(xsd_ready, c + 1)
                wait_emptied(dve, "ydiag", c)
                link(tt(ac, ac, xsd[b][:, :, 0:L], ALU.add))
                y = mix[:, 0:4, t0:t0 + L]
                if c == 0:
                    wait_emptied(dve, "z", 3, 1)
                tt(y, y, ac).then_inc(y_gated, 1)
                st8 = st.rearrange("p (h d) -> p h d", h=HEADS)
                wait_emptied(dve, "tot", c)
                if c >= 1:
                    wait_emptied(dve, "state", c - 1)
                link(tt(st8, st8, expo[:, b, HEADS:].unsqueeze(2).to_broadcast([P, HEADS, HD])))
                ps = wait_filled(dve, "state", c)
                tt(st, st, ps[:, :], ALU.add).then_inc(emptied["dve"], 1)
            ps = wait_filled(dve, "ssq")
            link(dve.memset(sstat[:, 0, :], 0.0))
            step(dve.tensor_copy(sstat[:, 0, 0:4], ps[:, 0:4]))
            dve.tensor_copy(sstat[0:NS, 0, 4:5], ps[0:NS, 4:5]).then_inc(emptied["dve"], 1)
            sync()
            wait_emptied(dve, "ssq")
            link(dve.tensor_scalar(sstat[:, 1, :], sstat[:, 0, :], 1.0 / SSD_W, EPS, ALU.mult, ALU.add))
            dve.reciprocal(sstat[:, 2, :], sstat[:, 1, :]).then_inc(small_ask, 1)
            for half in range(2):
                ps = wait_filled(dve, "rbc", half)
                lo, hi = (0, NP) if half == 0 else (NP, T)
                for i in range(4):
                    ins = dve.scalar_tensor_tensor(mix[:, i, lo:hi], mix[:, i, lo:hi], vecT[:, i, 5:6],
                                                   ps[:, 0:hi - lo], ALU.mult, ALU.mult)
                ins.then_inc(emptied["dve"], 1)
            wait_emptied(dve, "rbc", 1)
            dve.tensor_copy(sstat[:, 1, :], sstat[:, 2, :]).then_inc(mix_done, 1)

            def residual(stage, first, turned, g, t):
                L = TOK[t][1]
                for h in range(2):
                    ps = wait_filled(dve, stage, t, h)
                    x = H[0:L, t, 512 * h:512 * (h + 1)]
                    tt(x, x, ps[0:L, :], ALU.add).then_inc(emptied["dve"], 1)
                wait_emptied(dve, stage, t, 1)
                stats(first + t, H[0:L, t, :], L)
                if t >= 3:
                    wait_filled(dve, turned, t - 3, 1)
                    if first == NORM_F:
                        dve.wait_ge(f_stored[t % 3], 16)
                scale_rows(first + t, rows[0:L, t % 3, :], H[0:L, t, :], g, L)

            dve.wait_ge(h_loaded, 16 * NT)
            dve.wait_ge(gain_loaded[0], 32)
            wait_filled(dve, "memT", 1, 1)
            for t in range(NT):
                residual("out", NORM_H, "hT", 0, t)
            dve.wait_ge(gain_loaded[1], 32)
            for n_ in range(2 * NT + 1):
                if n_ < 2 * NT:
                    L, b = TOK[n_ % NT][1], n_ % 2
                    ps = wait_filled(dve, "score", n_)
                    dve.tensor_reduce(amax[0:L, n_, :], ps[0:L, :].rearrange("p (h m) -> p h m", h=2), AX.X, ALU.max,
                                      negate=True).then_inc(mx_ready, 1)
                    wait_emptied(dve, "score", n_)
                    link(dve.reciprocal(arec[0:L, n_, :], asum[0:L, n_, :]))
                    tt(PR[b][0:L], PR[b][0:L], arec[0:L, n_, :].unsqueeze(2).to_broadcast([L, 2, MEM]))\
                        .then_inc(pn_ready, 1)
                if n_ >= 1:
                    (t0, L), hp = TOK[(n_ - 1) % NT], (n_ - 1) // NT
                    ps = wait_filled(dve, "pv", n_ - 1)
                    copy_out(mix[:, 4 * hp:4 * hp + 4, t0:t0 + L],
                             ps[:, :].rearrange("p (i l) -> p i l", i=4)[:, :, 0:L])
                if n_ >= O_STEP:
                    residual("o", NORM_F, "fT", 1, n_ - O_STEP)
            residual("o", NORM_F, "fT", 1, NT - 1)

            dve.wait_ge(iota_ready, 1)
            step(dve.tensor_copy(slot_id, iot[:, 0:CAP]))
            step(dve.tensor_copy(tok_id, iot[:, CAP:CAP + NT]))
            step(dve.tensor_copy(prio, iot[:, CAP + NT:]))
            dve.wait_ge(route_loaded, 64)
            link(dve.memset(lg, 0.0))
            step(dve.memset(ind[:, NT, :], 0.0))
            step(dve.memset(before[:, 0, :], 0.0))

            def biased(ps, L, t_first, t_end):
                n_ = t_end - t_first
                return tt(lg[0:L, t_first:t_end, :],
                          ps[0:L, 36 * t_first:36 * t_end].rearrange("p (t e) -> p t e", t=n_),
                          b_rt[0:L, :].unsqueeze(1).to_broadcast([L, n_, NG + NE]), ALU.add)

            ps = wait_filled(dve, "route")
            step(biased(ps, P, 0, 4))
            biased(ps, NS, 4, NT).then_inc(emptied["dve"], 1)
            wait_emptied(dve, "route")

            def first_max(values, best, hot, work, n_):
                link(dve.tensor_reduce(best, values, AX.X, ALU.max))
                link(tt(work, values, best.to_broadcast([P, NT, n_]), ALU.is_equal))
                link(tt(work, work, prio[:, 0:n_].unsqueeze(1).to_broadcast([P, NT, n_])))
                link(dve.tensor_reduce(r_gs, work, AX.X, ALU.max))
                link(tt(hot, work, r_gs.to_broadcast([P, NT, n_]), ALU.is_equal))

            lgg = lg[:, :, 0:NG]
            first_max(lgg, r_gm, r_go, r_pr, NG)
            link(tt(r_gl, lgg, r_gm.to_broadcast([P, NT, NG]), ALU.subtract))
            full = r_full.rearrange("p t (g e) -> p t g e", g=NG)
            link(tt(full, lg[:, :, NG:].rearrange("p t (g e) -> p t g e", g=NG),
                    r_go.unsqueeze(3).to_broadcast([P, NT, NG, EG])))
            link(dve.tensor_reduce(r_sel, r_full.rearrange("p t (g e) -> p t e g", g=NG), AX.X, ALU.add))
            first_max(r_sel, r_m1, r_e1, r_eq, EG)
            link(dve.scalar_tensor_tensor(r_es, r_e1, -1e30, r_sel, ALU.mult, ALU.add))
            first_max(r_es, r_m2, r_e2, r_eq, EG)
            tt(r_d, r_m2, r_m1, ALU.subtract).then_inc(route_ask, 1)
            for dst, e_hot in ((ind1, r_e1), (ind2, r_e2)):
                step(tt(dst.rearrange("p t (g e) -> p t g e", g=NG), r_go.unsqueeze(3).to_broadcast([P, NT, NG, EG]),
                        e_hot.unsqueeze(2).to_broadcast([P, NT, NG, EG])))
            sync()
            for dst in (ind1, ind2):
                step(dve.memset(dst[NS:P, 4, :], 0.0))
            sync()
            link(tt(ind[:, 0:NT, :], ind1, ind2, ALU.add))
            for i in range(NT):
                link(tt(before[:, i + 1, :], before[:, i, :], ind[:, i, :], ALU.add))
            dve.tensor_copy(r_max, before[:, 0, 0:1]).then_inc(ind_ready, 1)
            for k, src in enumerate((ind1, ind2)):
                if k == 1:
                    link(dve.tensor_scalar(tok_id, tok_id, 1.0, None, ALU.add))
                link(tt(mv[k], src, tok_id.unsqueeze(2).to_broadcast([P, NT, NE])))
            ps = wait_filled(dve, "rank")
            rank_ps = ps[:, 0:NE * NT].rearrange("p (t e) -> p t e", t=NT)
            for src, dst in ((ind1, r_k1), (ind2, r_k2)):
                link(tt(r_full, src, rank_ps))
                link(dve.tensor_reduce(dst, r_full, AX.X, ALU.add))
            link(dve.tensor_reduce(r_max, ps[:, NE * NT:NE * (NT + 1)], AX.X, ALU.max))
            dve.tensor_scalar(flag[:, :], r_max, float(CAP), None, ALU.is_gt).then_inc(emptied["dve"], 1)
            wait_emptied(dve, "rank")

            def copy_x(pp, b):
                dve.wait_ge(turned_x, 4 * pp + (2 * b + 2))
                dve.tensor_copy(xgT[b][:, 4:8, :].rearrange("p k l -> p (k l)"), banks[1][:, 0:4 * CAP])\
                    .then_inc(xT_dve, 1)

            def dve_expert(pp, b, last=False, reused=True):
                dve.wait_ge(silu_done, 2 * pp + (b + 1))
                dve.wait_ge(gu_done, 2 * pp + (b + 1))
                tt(hid[b].rearrange("p j l -> p (j l)"), gact[b].rearrange("p j l -> p (j l)"),
                   banks[3][:, 0:2 * CAP]).then_inc(hid_ready, 1)
                if not last:
                    copy_x(pp + b, 1 - b)
                dve.wait_ge(dn_done, 4 * pp + (2 * b + 2))
                if reused:
                    dve.wait_ge(scattered[b], 16 * pp)
                dve.tensor_copy(yo[b][0:CAP, 512:D], banks[5 + 2 * b][0:CAP, :]).then_inc(yo_dve, 1)

            def expert_gates():
                dve.wait_ge(route_done, 1)
                link(dve.tensor_reduce(r_gs, r_gl, AX.X, ALU.add))
                link(dve.reciprocal(r_gp, r_gs))
                link(dve.tensor_scalar(r_e, r_d, 1.0, None, ALU.add))
                link(dve.reciprocal(r_gs, r_e))
                g1, g2_ = [gates[:, k, :].unsqueeze(2) for k in range(2)]
                link(tt(g1, r_gs, r_gp))
                link(tt(g2_, g1, r_d))

            def dve_pass(p):
                first = p * (LAST + 1)
                again = not isinstance(p, int)

                def link_table(ins, i):
                    ins.then_inc(table_step, 1)
                    dve.wait_ge(table_step, p * 4 + (i - 1 if again else i))

                if again:
                    dve.wait_ge(pass_done, p)
                    link_table(dve.tensor_scalar(slot_id, slot_id, float(CAP), None, ALU.add), 1)
                for k, rk in enumerate((r_k1, r_k2)):
                    m = tt(oh[k], slot_id.unsqueeze(1).to_broadcast([P, NT, CAP]), rk.to_broadcast([P, NT, CAP]),
                           ALU.is_equal)
                m.then_inc(oh_ready, 1)
                if not again:
                    expert_gates()
                dve.wait_ge(slots_filled, p + 1)
                v = banks[0][0:CAP, 0:NE]
                link_table(dve.tensor_scalar(idx_f[0:CAP, 0, :], v, 0.0, SKIP, ALU.is_equal, ALU.mult), 1 + again)
                link_table(tt(idx_f[0:CAP, 1, :], idx_f[0:CAP, 0, :], v, ALU.add), 2 + again)
                link_table(dve.tensor_scalar(idx_y[0:CAP, :], idx_f[0:CAP, 1, :], -1.0, None, ALU.add), 3 + again)
                dve.tensor_scalar(idx_x[0:CAP, :], idx_y[0:CAP, :], 1, None, ALU.arith_shift_right)\
                    .then_inc(idx_ready, 1)
                copy_x(first, 0)
                for b in range(2):
                    dve_expert(first, b, reused=again)
                with dve.Fori(1, LAST) as i:
                    for b in range(2):
                        dve_expert(first + i, b)
                for b in range(2):
                    dve_expert(first + LAST, b, last=(b == 1))

            dve_pass(0)
            overflow_passes(dve, dve_pass)

            def final_rows(t):
                L, k = TOK[t][1], NORM_Y + t
                dve.wait_ge(rstd_ready, k + 1)
                dve.scalar_tensor_tensor(y2[t][0:L, 1, :], H[0:L, t, :], stat[0:L, k, 16:17], gain[0:L, 0, :],
                                         ALU.mult, ALU.mult).then_inc(y_normed, 1)

            dve.wait_ge(gain_loaded[0], 48)
            for t in range(NT + 1):
                if t < NT:
                    L = TOK[t][1]
                    dve.wait_ge(y2_loaded[t], 16)
                    dve.scalar_tensor_tensor(H[0:L, t, :], y2[t][0:L, 0, :], gates[0:L, 0, t:t + 1], H[0:L, t, :],
                                             ALU.mult, ALU.add).then_inc(y2_added, 1)
                    dve.wait_ge(y2_added, t + 1)
                    dve.scalar_tensor_tensor(H[0:L, t, :], y2[t][0:L, 1, :], gates[0:L, 1, t:t + 1], H[0:L, t, :],
                                             ALU.mult, ALU.add).then_inc(h_final, 1)
                if t >= 1:
                    L, k = TOK[t - 1][1], NORM_Y + t - 1
                    dve.wait_ge(h_squared, t)
                    link(dve.tensor_scalar(stat[0:L, k, 17:18], stat[0:L, k, 14:15], 1.0 / D, EPS, ALU.mult, ALU.add))
                    dve.reciprocal(stat[0:L, k, 15:16], stat[0:L, k, 17:18]).then_inc(ms_ready, 1)
            for t in range(Y_POOL, NT):
                final_rows(t)


def kernel(**inputs):
    import numpy as np
    import concourse.bacc as bacc
    from concourse.bass_utils import run_bass_kernel_spmd

    nc = bacc.Bacc("TRN2", target_bir_lowering=False, num_devices=1)
    arrays, a, o = {}, {}, {}
    for name in IN:
        x = np.ascontiguousarray(inputs[name])
        arrays[f"in_{name}"] = x
        a[name] = nc.dram_tensor(f"in_{name}", x.shape, mybir.dt.from_np(x.dtype), kind="ExternalInput").ap()
    for name, shape in OUT:
        o[name] = nc.dram_tensor(f"out_{name}", shape, F32, kind="ExternalOutput").ap()
    build(nc, a, o)
    r = run_bass_kernel_spmd(nc, [arrays], core_ids=[0])
    return tuple(r.results[0][f"out_{name}"] for name, _ in OUT)
```
